# Optimizing a Trainium2 kernel written in Bass

```python
import jax, jax.numpy as jnp
from jax import lax
import numpy as np
import math

D_MODEL = 1024
BATCH = 1
SEQ = 256
DEPTH = 2

HEAD_DIM = 64
BLOCK = 128
A_Q_HEADS = 8
A_KV_HEADS = 2
A_WINDOW = 128
B_Q_HEADS = 8
B_KV_HEADS = 2
CMP_LEN = 32
CMP_STRIDE = 16
CMP_HIDDEN = 128
SLC_LEN = 64
N_SLC = 16
N_LOCAL_SLC = 2
B_WINDOW = 512
D_FF = 2816
CONV_WIDTH = 3
ROPE_THETA = 10000.0
EPS = 1e-6
TINY = 1e-30

A_WIDTH = A_Q_HEADS * HEAD_DIM
A_KV_WIDTH = A_KV_HEADS * HEAD_DIM
B_WIDTH = B_Q_HEADS * HEAD_DIM
B_KV_WIDTH = B_KV_HEADS * HEAD_DIM
N_NSA_GATES = 3 * B_Q_HEADS
IN_SIZES = (A_WIDTH, A_KV_WIDTH, A_KV_WIDTH,
            B_WIDTH, B_KV_WIDTH, B_KV_WIDTH, B_KV_WIDTH, B_KV_WIDTH, B_KV_WIDTH, B_KV_WIDTH,
            N_NSA_GATES, D_MODEL, D_MODEL)
IN_COLS = sum(IN_SIZES)


def rms_norm(x, gain):
    xf = x.astype(jnp.float32)
    y = xf * lax.rsqrt(jnp.mean(xf * xf, axis=-1, keepdims=True) + EPS)
    return (y * gain.astype(jnp.float32)).astype(x.dtype)

def apply_rope(x, positions):
    half = HEAD_DIM // 2
    inv_freq = ROPE_THETA ** (-jnp.arange(half, dtype=jnp.float32) / half)
    ang = positions.astype(jnp.float32)[..., None] * inv_freq
    cos = jnp.cos(ang)[:, :, None, :]
    sin = jnp.sin(ang)[:, :, None, :]
    xf = x.astype(jnp.float32)
    x1, x2 = xf[..., :half], xf[..., half:]
    return jnp.concatenate([x1 * cos - x2 * sin, x2 * cos + x1 * sin], axis=-1).astype(x.dtype)

def masked_softmax(s, mask):
    s = jnp.where(mask, s, -jnp.inf)
    m = jnp.max(s, axis=-1, keepdims=True)
    m = jnp.where(jnp.isfinite(m), m, 0.0)
    p = jnp.exp(s - m)
    return p / jnp.maximum(jnp.sum(p, axis=-1, keepdims=True), TINY)

def band_context(t, n_prev):
    nb = t.shape[1]
    pad = [(0, 0)] * t.ndim
    pad[1] = (n_prev, 0)
    tp = jnp.pad(t, pad)
    return jnp.concatenate([tp[:, j:j + nb] for j in range(n_prev + 1)], axis=2)

def swa_sink_attention(q, k, v, sinks):
    b, s, g, r, d = q.shape
    nb = s // BLOCK
    n_prev = -(-A_WINDOW // BLOCK)
    qb = q.reshape(b, nb, BLOCK, g, r, d)
    kc = band_context(k.reshape(b, nb, BLOCK, g, d), n_prev)
    vc = band_context(v.reshape(b, nb, BLOCK, g, d), n_prev)
    scores = jnp.einsum('bnqgrd,bnkgd->bngrqk', qb, kc).astype(jnp.float32) * (d ** -0.5)
    blk = jnp.arange(nb)[:, None, None] * BLOCK
    qpos = blk + jnp.arange(BLOCK)[None, :, None]
    kpos = blk - n_prev * BLOCK + jnp.arange((n_prev + 1) * BLOCK)[None, None, :]
    rel = qpos - kpos
    mask = (rel >= 0) & (rel < A_WINDOW) & (kpos >= 0)
    scores = jnp.where(mask[None, :, None, None], scores, -jnp.inf)
    sink = sinks.astype(jnp.float32).reshape(1, 1, g, r, 1, 1)
    m = jnp.maximum(jnp.max(scores, axis=-1, keepdims=True), sink)
    p = jnp.exp(scores - m)
    p = p / (jnp.sum(p, axis=-1, keepdims=True) + jnp.exp(sink - m))
    o = jnp.einsum('bngrqk,bnkgd->bnqgrd', p.astype(v.dtype), vc)
    return o.reshape(b, s, g * r * d)

def compress(t, pos_emb, w1, b1, w2):
    b, s, g, d = t.shape
    ratio = CMP_LEN // CMP_STRIDE
    chunks = t.reshape(b, s // CMP_STRIDE, CMP_STRIDE, g, d)
    nc = s // CMP_STRIDE - ratio + 1
    blocks = jnp.concatenate([chunks[:, j:j + nc] for j in range(ratio)], axis=2)
    blocks = blocks + pos_emb[None, None, :, None, :]
    flat = blocks.transpose(0, 1, 3, 2, 4).reshape(b, nc, g, CMP_LEN * d)
    hid = jax.nn.gelu(flat @ w1 + b1, approximate=True)
    return hid @ w2

def nsa_attention(q_raw, q_rot, k_cmp, v_cmp, k_slc, v_slc, k_win, v_win, gates):
    b, s, g, r, d = q_rot.shape
    nb = s // BLOCK
    nc = k_cmp.shape[1]
    ns = s // SLC_LEN
    n_sel = min(N_SLC, ns)
    scale = d ** -0.5
    ratio_c = CMP_LEN // CMP_STRIDE
    ratio_s = SLC_LEN // CMP_STRIDE
    ks_blocks = k_slc.reshape(b, ns, SLC_LEN, g, d).transpose(0, 3, 1, 2, 4)
    vs_blocks = v_slc.reshape(b, ns, SLC_LEN, g, d).transpose(0, 3, 1, 2, 4)
    kw_pad = jnp.pad(k_win, ((0, 0), (B_WINDOW, 0), (0, 0), (0, 0)))
    vw_pad = jnp.pad(v_win, ((0, 0), (B_WINDOW, 0), (0, 0), (0, 0)))
    cmp_end = jnp.arange(nc) * CMP_STRIDE + CMP_LEN - 1
    blk_ids = jnp.arange(ns)
    gather = jax.vmap(jax.vmap(lambda blocks, ix: blocks[ix]))

    def one_block(i):
        start = i * BLOCK
        t = start + jnp.arange(BLOCK)
        qr = lax.dynamic_slice_in_dim(q_rot, start, BLOCK, axis=1)
        qn = lax.dynamic_slice_in_dim(q_raw, start, BLOCK, axis=1)
        gt = lax.dynamic_slice_in_dim(gates, start, BLOCK, axis=1)
        s_c = jnp.einsum('bqgrd,bcgd->bgrqc', qn, k_cmp).astype(jnp.float32) * scale
        p_c = masked_softmax(s_c, cmp_end[None, :] <= t[:, None])
        o_c = jnp.einsum('bgrqc,bcgd->bqgrd', p_c.astype(v_cmp.dtype), v_cmp)
        imp = jnp.sum(p_c, axis=2)
        imp = jnp.pad(imp, ((0, 0), (0, 0), (0, 0), (ratio_c - 1, ratio_s * ns - nc)))
        imp_s = jnp.zeros(imp.shape[:-1] + (ns,), jnp.float32)
        for m in range(ratio_s):
            for n in range(ratio_c):
                off = m - n + ratio_c - 1
                imp_s = imp_s + imp[..., off:off + ratio_s * ns:ratio_s]
        cur = t // SLC_LEN
        valid = blk_ids[None, :] <= cur[:, None]
        forced = (blk_ids[None, :] == 0) | (valid & (blk_ids[None, :] > cur[:, None] - N_LOCAL_SLC))
        imp_s = jnp.where(forced, jnp.inf, jnp.where(valid, imp_s, -jnp.inf))
        _, idx = lax.top_k(imp_s, n_sel)
        k_sel = gather(ks_blocks, idx)
        v_sel = gather(vs_blocks, idx)
        s_s = jnp.einsum('bqgrd,bgqkld->bgrqkl', qr, k_sel).astype(jnp.float32) * scale
        tok = idx[..., None] * SLC_LEN + jnp.arange(SLC_LEN)
        mask_s = (tok <= t[None, None, :, None, None]).reshape(b, g, 1, BLOCK, n_sel * SLC_LEN)
        p_s = masked_softmax(s_s.reshape(b, g, r, BLOCK, n_sel * SLC_LEN), mask_s)
        o_s = jnp.einsum('bgrqn,bgqnd->bqgrd', p_s.astype(v_slc.dtype),
                         v_sel.reshape(b, g, BLOCK, n_sel * SLC_LEN, d))
        kwin = lax.dynamic_slice_in_dim(kw_pad, start, BLOCK + B_WINDOW, axis=1)
        vwin = lax.dynamic_slice_in_dim(vw_pad, start, BLOCK + B_WINDOW, axis=1)
        kpos = start - B_WINDOW + jnp.arange(BLOCK + B_WINDOW)
        rel = t[:, None] - kpos[None, :]
        mask_w = (rel >= 0) & (rel < B_WINDOW) & (kpos[None, :] >= 0)
        s_w = jnp.einsum('bqgrd,bkgd->bgrqk', qr, kwin).astype(jnp.float32) * scale
        p_w = masked_softmax(s_w, mask_w)
        o_w = jnp.einsum('bgrqk,bkgd->bqgrd', p_w.astype(v_win.dtype), vwin)
        return gt[..., 0:1] * o_c + gt[..., 1:2] * o_s + gt[..., 2:3] * o_w

    out = lax.map(one_block, jnp.arange(nb))
    return out.transpose(1, 0, 2, 3, 4, 5).reshape(b, s, g * r * d)

def conv_ffn(h, w_up, conv_w, conv_b, w_down):
    u = h @ w_up
    s = u.shape[1]
    up = jnp.pad(u, ((0, 0), (CONV_WIDTH - 1, 0), (0, 0)))
    c = conv_b
    for k in range(CONV_WIDTH):
        c = c + conv_w[k] * up[:, k:k + s]
    a, val = jnp.split(c, 2, axis=-1)
    return (jax.nn.gelu(a, approximate=True) * val) @ w_down

def hybrid_layer(x, positions, attn_pre_gain, attn_post_gain, ffn_pre_gain, ffn_post_gain,
                 w_in, attn_sinks, cmp_pos_emb, cmp_w1, cmp_b1, cmp_w2,
                 w_branch_a, w_branch_b, w_out, ffn_w_up, ffn_conv_w, ffn_conv_b, ffn_w_down):
    b, s, _ = x.shape
    hd = HEAD_DIM
    h = rms_norm(x, attn_pre_gain)
    u = h @ w_in
    offsets = np.cumsum(np.array(IN_SIZES))[:-1].tolist()
    (qa, ka, va, qb, kcb, vcb, ksb, vsb, kwb, vwb, g_nsa, g_a, g_b) = jnp.split(u, offsets, axis=-1)
    ra = A_Q_HEADS // A_KV_HEADS
    qa = apply_rope(qa.reshape(b, s, A_Q_HEADS, hd), positions).reshape(b, s, A_KV_HEADS, ra, hd)
    ka = apply_rope(ka.reshape(b, s, A_KV_HEADS, hd), positions)
    va = va.reshape(b, s, A_KV_HEADS, hd)
    o_a = swa_sink_attention(qa, ka, va, attn_sinks)
    rb = B_Q_HEADS // B_KV_HEADS
    qb = qb.reshape(b, s, B_Q_HEADS, hd)
    qb_rot = apply_rope(qb, positions).reshape(b, s, B_KV_HEADS, rb, hd)
    qb_raw = qb.reshape(b, s, B_KV_HEADS, rb, hd)
    kc = compress(kcb.reshape(b, s, B_KV_HEADS, hd), cmp_pos_emb[0], cmp_w1[0], cmp_b1[0], cmp_w2[0])
    vc = compress(vcb.reshape(b, s, B_KV_HEADS, hd), cmp_pos_emb[1], cmp_w1[1], cmp_b1[1], cmp_w2[1])
    ks = apply_rope(ksb.reshape(b, s, B_KV_HEADS, hd), positions)
    kw = apply_rope(kwb.reshape(b, s, B_KV_HEADS, hd), positions)
    vs = vsb.reshape(b, s, B_KV_HEADS, hd)
    vw = vwb.reshape(b, s, B_KV_HEADS, hd)
    gates = jax.nn.sigmoid(g_nsa).reshape(b, s, B_KV_HEADS, rb, 3)
    o_b = nsa_attention(qb_raw, qb_rot, kc, vc, ks, vs, kw, vw, gates)
    mixed = jax.nn.sigmoid(g_a) * (o_a @ w_branch_a) + jax.nn.sigmoid(g_b) * (o_b @ w_branch_b)
    x = x + rms_norm(mixed @ w_out, attn_post_gain)
    h = rms_norm(x, ffn_pre_gain)
    x = x + rms_norm(conv_ffn(h, ffn_w_up, ffn_conv_w, ffn_conv_b, ffn_w_down), ffn_post_gain)
    return x

def first_inputs(seed: int = 0) -> dict:
    key = jax.random.key(seed)
    ks = jax.random.split(key, 20)
    f32 = jnp.float32

    def nrm(k, shape, scale):
        return scale * jax.random.normal(k, shape, f32)

    x = nrm(ks[0], (BATCH, SEQ, D_MODEL), 1.0)
    positions = jnp.broadcast_to(jnp.arange(SEQ, dtype=jnp.int32)[None, :], (BATCH, SEQ))
    return {
        'x': x,
        'positions': positions,
        'attn_pre_gain': 1.0 + nrm(ks[1], (DEPTH, D_MODEL), 0.05),
        'attn_post_gain': 1.0 + nrm(ks[2], (DEPTH, D_MODEL), 0.05),
        'ffn_pre_gain': 1.0 + nrm(ks[3], (DEPTH, D_MODEL), 0.05),
        'ffn_post_gain': 1.0 + nrm(ks[4], (DEPTH, D_MODEL), 0.05),
        'w_in': nrm(ks[5], (DEPTH, D_MODEL, IN_COLS), D_MODEL ** -0.5),
        'attn_sinks': nrm(ks[6], (DEPTH, A_Q_HEADS), 1.0),
        'cmp_pos_emb': nrm(ks[7], (DEPTH, 2, CMP_LEN, HEAD_DIM), 0.1),
        'cmp_w1': nrm(ks[8], (DEPTH, 2, CMP_LEN * HEAD_DIM, CMP_HIDDEN), (CMP_LEN * HEAD_DIM) ** -0.5),
        'cmp_b1': nrm(ks[9], (DEPTH, 2, CMP_HIDDEN), 0.01),
        'cmp_w2': nrm(ks[10], (DEPTH, 2, CMP_HIDDEN, HEAD_DIM), CMP_HIDDEN ** -0.5),
        'w_branch_a': nrm(ks[11], (DEPTH, A_WIDTH, D_MODEL), A_WIDTH ** -0.5),
        'w_branch_b': nrm(ks[12], (DEPTH, B_WIDTH, D_MODEL), B_WIDTH ** -0.5),
        'w_out': nrm(ks[13], (DEPTH, D_MODEL, D_MODEL), D_MODEL ** -0.5),
        'ffn_w_up': nrm(ks[14], (DEPTH, D_MODEL, 2 * D_FF), D_MODEL ** -0.5),
        'ffn_conv_w': nrm(ks[15], (DEPTH, CONV_WIDTH, 2 * D_FF), CONV_WIDTH ** -0.5),
        'ffn_conv_b': nrm(ks[16], (DEPTH, 2 * D_FF), 0.01),
        'ffn_w_down': nrm(ks[17], (DEPTH, D_FF, D_MODEL), D_FF ** -0.5),
    }

def first_block(x, positions, attn_pre_gain, attn_post_gain, ffn_pre_gain, ffn_post_gain,
              w_in, attn_sinks, cmp_pos_emb, cmp_w1, cmp_b1, cmp_w2,
              w_branch_a, w_branch_b, w_out, ffn_w_up, ffn_conv_w, ffn_conv_b, ffn_w_down):
    for l in range(DEPTH):
        x = hybrid_layer(x, positions, attn_pre_gain[l], attn_post_gain[l], ffn_pre_gain[l],
                         ffn_post_gain[l], w_in[l], attn_sinks[l], cmp_pos_emb[l], cmp_w1[l],
                         cmp_b1[l], cmp_w2[l], w_branch_a[l], w_branch_b[l], w_out[l],
                         ffn_w_up[l], ffn_conv_w[l], ffn_conv_b[l], ffn_w_down[l])
    return x


MIX_WIDTH = D_MODEL
ATTN_HEADS = 8
ATTN_HEAD_DIM = 64
ATTN_DIM = ATTN_HEADS * ATTN_HEAD_DIM
CONV_DIM = D_MODEL // 4
POOL_WINDOWS = (2, 4, 8, 16)
N_POOL_GROUPS = len(POOL_WINDOWS)
POOL_DIM = D_MODEL // 4
POOL_GD = POOL_DIM // N_POOL_GROUPS
Q_BLOCK = 128
RMS_EPS = 1e-6
SPLIT_SIZES = (ATTN_DIM, ATTN_DIM, ATTN_DIM, CONV_DIM, CONV_DIM, CONV_DIM, POOL_DIM)
IN_PROJ_WIDTH = sum(SPLIT_SIZES)
SPLIT_POINTS = tuple(int(v) for v in np.cumsum(SPLIT_SIZES)[:-1])


def _rmsnorm(x, g):
    x32 = x.astype(jnp.float32)
    y = x32 * lax.rsqrt(jnp.mean(x32 * x32, axis=-1, keepdims=True) + RMS_EPS)
    return (y * g.astype(jnp.float32)).astype(x.dtype)

def _swiglu(h, w_gate, w_up, w_down):
    return (jax.nn.silu(h @ w_gate) * (h @ w_up)) @ w_down

def _stick_breaking_attention(q, k, v):
    B, S, H, dh = q.shape
    nb = S // Q_BLOCK
    scale = 1.0 / math.sqrt(dh)
    kh = k.transpose(0, 2, 1, 3)
    vh = v.transpose(0, 2, 1, 3)
    q_blocks = q.transpose(0, 2, 1, 3).reshape(B, H, nb, Q_BLOCK, dh).transpose(2, 0, 1, 3, 4)
    k_pos = jnp.arange(S)

    def block(args):
        q_blk, start = args
        q_pos = start + jnp.arange(Q_BLOCK)
        z = jnp.einsum('bhqd,bhkd->bhqk', q_blk, kh).astype(jnp.float32) * scale
        mask = k_pos[None, :] < q_pos[:, None]
        log_keep = jnp.where(mask, jax.nn.log_sigmoid(-z), 0.0)
        between = lax.cumsum(log_keep, axis=3, reverse=True) - log_keep
        a = jnp.where(mask, jnp.exp(jax.nn.log_sigmoid(z) + between), 0.0)
        return jnp.einsum('bhqk,bhkd->bhqd', a.astype(vh.dtype), vh)

    out = lax.map(block, (q_blocks, jnp.arange(nb) * Q_BLOCK))
    return out.transpose(1, 0, 3, 2, 4).reshape(B, S, H * dh)

def _short_conv(gate_b, gate_c, h, conv_w):
    S = h.shape[1]
    u = gate_c * h
    u_pad = jnp.pad(u, ((0, 0), (CONV_WIDTH - 1, 0), (0, 0)))
    y = conv_w[0] * u_pad[:, 0:S] + conv_w[1] * u_pad[:, 1:S + 1] + conv_w[2] * u_pad[:, 2:S + 2]
    return gate_b * y

def _multiscale_pool(p, pool_w, pool_scale):
    B, S, C = p.shape
    p32 = p.astype(jnp.float32).reshape(B, S, N_POOL_GROUPS, POOL_GD)
    cs0 = jnp.pad(jnp.cumsum(p32, axis=1), ((0, 0), (1, 0), (0, 0), (0, 0)))
    count_base = jnp.arange(1, S + 1, dtype=jnp.float32)
    outs = []
    for gi, w in enumerate(POOL_WINDOWS):
        lagged = jnp.pad(cs0[:, :S + 1 - w, gi], ((0, 0), (w - 1, 0), (0, 0)))
        mean = (cs0[:, 1:, gi] - lagged) / jnp.minimum(count_base, w)[None, :, None]
        outs.append(mean - p32[:, :, gi])
    d = jnp.stack(outs, axis=2).astype(p.dtype)
    y = jnp.einsum('bsgc,gcd->bsgd', d, pool_w).reshape(B, S, C)
    return y * pool_scale

def _mixer(h, w_in, conv_w, pool_w, pool_scale, w_out):
    B, S, _ = h.shape
    proj = h @ w_in
    q, k, v, gate_b, gate_c, conv_h, pool_in = jnp.split(proj, SPLIT_POINTS, axis=-1)
    q = q.reshape(B, S, ATTN_HEADS, ATTN_HEAD_DIM)
    k = k.reshape(B, S, ATTN_HEADS, ATTN_HEAD_DIM)
    v = v.reshape(B, S, ATTN_HEADS, ATTN_HEAD_DIM)
    attn = _stick_breaking_attention(q, k, v)
    conv = _short_conv(gate_b, gate_c, conv_h, conv_w)
    pool = _multiscale_pool(pool_in, pool_w, pool_scale)
    return jnp.concatenate([attn, conv, pool], axis=-1) @ w_out

def second_inputs(seed: int = 0) -> dict:
    key = jax.random.key(seed)
    ks = jax.random.split(key, 11)
    f32 = jnp.float32
    x = jax.random.normal(ks[0], (BATCH, SEQ, D_MODEL), f32)
    norm_g = 1.0 + 0.05 * jax.random.normal(ks[1], (DEPTH, 6, D_MODEL), f32)
    ffn_w_gate = jax.random.normal(ks[2], (DEPTH, 2, D_MODEL, D_FF), f32) * D_MODEL ** -0.5
    ffn_w_up = jax.random.normal(ks[3], (DEPTH, 2, D_MODEL, D_FF), f32) * D_MODEL ** -0.5
    ffn_w_down = jax.random.normal(ks[4], (DEPTH, 2, D_FF, D_MODEL), f32) * D_FF ** -0.5
    w_in = jax.random.normal(ks[5], (DEPTH, D_MODEL, IN_PROJ_WIDTH), f32) * D_MODEL ** -0.5
    conv_w = jax.random.normal(ks[6], (DEPTH, CONV_WIDTH, CONV_DIM), f32) * CONV_WIDTH ** -0.5
    pool_w = jax.random.normal(ks[7], (DEPTH, N_POOL_GROUPS, POOL_GD, POOL_GD), f32) * POOL_GD ** -0.5
    pool_scale = 1.0 + 0.05 * jax.random.normal(ks[8], (DEPTH, POOL_DIM), f32)
    w_out = jax.random.normal(ks[9], (DEPTH, MIX_WIDTH, D_MODEL), f32) * MIX_WIDTH ** -0.5
    return {"x": x, "norm_g": norm_g, "ffn_w_gate": ffn_w_gate, "ffn_w_up": ffn_w_up,
            "ffn_w_down": ffn_w_down, "w_in": w_in, "conv_w": conv_w, "pool_w": pool_w,
            "pool_scale": pool_scale, "w_out": w_out}

def second_block(x, norm_g, ffn_w_gate, ffn_w_up, ffn_w_down, w_in, conv_w, pool_w, pool_scale, w_out):
    for l in range(DEPTH):
        g = norm_g[l]
        f = _swiglu(_rmsnorm(x, g[0]), ffn_w_gate[l, 0], ffn_w_up[l, 0], ffn_w_down[l, 0])
        x = x + 0.5 * _rmsnorm(f, g[1])
        m = _mixer(_rmsnorm(x, g[2]), w_in[l], conv_w[l], pool_w[l], pool_scale[l], w_out[l])
        x = x + _rmsnorm(m, g[3])
        f = _swiglu(_rmsnorm(x, g[4]), ffn_w_gate[l, 1], ffn_w_up[l, 1], ffn_w_down[l, 1])
        x = x + 0.5 * _rmsnorm(f, g[5])
    return x


def setup_inputs(seed=0):
    out = dict(first_inputs(seed))
    for name, value in second_inputs(seed + 1).items():
        if name != "x":
            out[name + "_2"] = value
    return out


def reference(
    x, positions, attn_pre_gain, attn_post_gain, ffn_pre_gain, ffn_post_gain, w_in, attn_sinks,
    cmp_pos_emb, cmp_w1, cmp_b1, cmp_w2, w_branch_a, w_branch_b, w_out, ffn_w_up, ffn_conv_w,
    ffn_conv_b, ffn_w_down, norm_g_2, ffn_w_gate_2, ffn_w_up_2, ffn_w_down_2, w_in_2, conv_w_2,
    pool_w_2, pool_scale_2, w_out_2,
):
    x = first_block(
        x, positions, attn_pre_gain, attn_post_gain, ffn_pre_gain, ffn_post_gain, w_in,
        attn_sinks, cmp_pos_emb, cmp_w1, cmp_b1, cmp_w2, w_branch_a, w_branch_b, w_out,
        ffn_w_up, ffn_conv_w, ffn_conv_b, ffn_w_down,
    )
    return second_block(
        x, norm_g_2, ffn_w_gate_2, ffn_w_up_2, ffn_w_down_2, w_in_2, conv_w_2, pool_w_2,
        pool_scale_2, w_out_2,
    )


_drawn_inputs = setup_inputs


def setup_inputs(seed=0):
    import zlib

    import numpy as np

    out = dict(_drawn_inputs(seed))
    spreads = {}
    factors = {'cmp_b1': 4.194, 'ffn_conv_b': 3.927, 'pool_scale_2': 4.378}
    for name, (base, spread) in spreads.items():
        noise = np.random.default_rng([zlib.crc32(name.encode()), seed]).standard_normal(out[name].shape)
        drawn = base * np.exp(spread * noise) if base else spread * noise
        out[name] = __import__('jax').numpy.asarray(drawn.astype(out[name].dtype))
    for name, factor in factors.items():
        out[name] = (out[name] * factor).astype(out[name].dtype)
    return out
```

```python
from contextlib import ExitStack

import numpy as np

import concourse.bass as bass
from concourse import mybir

F32 = mybir.dt.float32
F32R = mybir.dt.float32r
I32 = mybir.dt.int32
ALU = mybir.AluOpType
ACT = mybir.ActivationFunctionType
AX_X = mybir.AxisListType.X
ds = bass.ds

P = 128
S = 256
D = 1024
KD = D // P
DEPTH = 2
FF = 2816
KF = FF // P
HD = 64
EPS = 1e-6
TINY = 1e-30
NEG = -1e30
SCALE = HD ** -0.5
GATE_COL = 2048
GA_COL = GATE_COL + 24
N_CMP = 15
HALF_K = KF // 2
CH = 2048
CH_DOWN = HALF_K * P
RING = 4
TWO_PI = 2.0 * np.pi
PI_A = 6.28125
PI_B = float(np.float32(np.round((TWO_PI - PI_A) * 2.0 ** 20) / 2.0 ** 20))
PI_C = float(np.float32(TWO_PI - PI_A - PI_B))
ROUND = 12582912.0
PI_MAX = 3.1415925

CHUNKS_1 = 8 + 2 + 8 + 4 + 4 + 22 + 16
CHUNKS_2 = 22 + 16 + 10 + 4 + 22 + 16

CONST = {"ident": 128, "swap": 128, "ntri": 128, "stick": 128, "mask_a": 256, "mask_c": 256,
         "mask_cmp": 32, "count": 32, "width": 2, "freq": 1, "sign": 1}
CONST_AT, _n = {}, 0
for _k, _w in CONST.items():
    CONST_AT[_k] = (_n, _w)
    _n += _w
CONST_COLS = _n


def host_constants():
    c = np.zeros((P, CONST_COLS), np.float32)

    def put(name, a):
        at, w = CONST_AT[name]
        c[:, at:at + w] = np.asarray(a, np.float32).reshape(P, w)
    i = np.arange(P)
    put("ident", np.eye(P))
    put("swap", (i[:, None] == (i ^ 32)[None, :]))
    put("ntri", np.where(i[:, None] >= i[None, :], -1.0, 0.0))
    put("stick", np.where(i[:, None] < i[None, :], 0.0, NEG))
    tri = np.where(i[None, :] <= i[:, None], 0.0, NEG)
    put("mask_a", np.concatenate([np.where(i[None, :] > i[:, None], 0.0, NEG), tri], 1))
    put("mask_c", np.concatenate([np.zeros((P, P)), tri], 1))
    end = np.arange(16) * 16 + 31
    end[15] = 1 << 20
    t = np.stack([i, i + P], 1)
    put("mask_cmp", np.where(end[None, None, :] <= t[:, :, None], 0.0, NEG))
    width = np.where(i[:, None] < 64, [[2, 8]], [[4, 16]])
    put("count", 1.0 / np.minimum(np.arange(1, 17)[None, None, :], width[:, :, None]))
    put("width", 1.0 / width)
    put("freq", np.float32(10000.0) ** (-(i % 32).astype(np.float32) / np.float32(32)))
    put("sign", np.where(i % 64 < 32, -1.0, 1.0))
    return c


T1 = {"in": 0, "cmp": 16, "branch": 18, "out": 50, "up": 58, "down": 102}
T2 = {"up0": 0, "down0": 44, "in": 52, "out": 72, "up1": 80, "down1": 124}
C1 = {"in": 0, "cmp": 8, "branch": 10, "out": 22, "up": 26, "down": 48}
C2 = {"up0": 0, "down0": 22, "in": 38, "out": 48, "up1": 52, "down1": 74}
PER_SLOT = {1: [CHUNKS_1 // RING] * RING, 2: [(CHUNKS_2 + RING - 1 - n) // RING for n in range(RING)]}
SIZES = {1: [CH] * C1["down"] + [CH_DOWN] * 16,
         2: [CH] * 22 + [CH_DOWN] * 16 + [CH] * 36 + [CH_DOWN] * 16}
CUT = {CH: ((0, CH // 2), (CH // 2, CH)), CH_DOWN: ((0, 6 * P), (6 * P, CH_DOWN))}

QA, KA, KS, KW, VW, QB, KCB, VCB, VA, VS = 0, 4, 5, 6, 7, 8, 12, 13, 14, 15
PLACE = [QA, QA + 1, QA + 2, QA + 3, KA, VA, QB, QB + 1, QB + 2, QB + 3, KCB, VCB, KS, VS, KW, VW]
ROPE = [0, 1, 2, 3, 4, 6, 7, 8, 9, 12, 14]
VALS = [5, 13, 15]
KEYS = [(4, KA), (12, KS), (14, KW)]

UNITS = [(g, qb, hs) for g in range(2) for qb, hs in
         ((0, [4 * g + r for r in range(4)]), (1, [4 * g, 4 * g + 1]), (1, [4 * g + 2, 4 * g + 3]))]
MAPS = [(u, 0) for u in range(6)] + [(u, b) for u in range(6) for b in (1, 2)]
LAST_MAP = list(range(6)) + [7 + 2 * u for u in range(6)]


def build(nc, a, out):
    ctx = ExitStack()
    top = [(nc.sbuf_base + 31) // 32 * 32]

    def sb(name, shape, dt=F32, at=None):
        size = (int(np.prod(shape[1:])) * 4 + 31) // 32 * 32
        if at is None:
            at = top[0]
            top[0] += size
        return nc.alloc_sbuf_tensor_at(name, list(shape), dt, offset=at), at, at + size

    raw = sb("raw", [P, RING, CH])[0]
    whi = [sb(f"whi{n}", [P, CH], F32R)[0] for n in range(RING)]
    wlo = [sb(f"wlo{n}", [P, CH], F32R)[0] for n in range(RING)]
    hsA = sb("hsA", [P, KD, 2 * S], F32R)[0]
    hsB, hsB_at, hsB_end = sb("hsB", [P, KD, 2 * S], F32R)
    hid, ws_at, ws_end = sb("hid", [P, KF, 2 * S], F32R)
    xT = sb("xT", [P, KD, S])[0]
    low, low_at, _ = sb("low", [P, 4, S])
    sq = sb("sq", [P, 2, S])[0]
    sqsum = sb("sqsum", [P, S])[0]
    rstd = sb("rstd", [P, S])[0]
    tm = sb("tm", [P, 2, S])[0]
    cosT = sb("cosT", [P, S])[0]
    sinT = sb("sinT", [P, S])[0]
    const = sb("const", [P, CONST_COLS])[0]
    mean_w = sb("mean_w", [P, P])[0]
    nones = sb("nones", [P, P])[0]
    col = sb("col", [P, 2])[0]
    gainT = sb("gainT", [P, 180])[0]
    convT = sb("convT", [P, 4, 88])[0]
    posT = sb("posT", [P, P])[0]
    w2all = sb("w2all", [P, DEPTH, 2, HD])[0]
    w2cur = sb("w2cur", [P, 2, 2, HD])[0]
    wg = sb("wg", [P, DEPTH, KD, 24])[0]
    sink = sb("sink", [P, DEPTH, 8])[0]
    nsink = sb("nsink", [P, DEPTH, 8])[0]
    poolw = sb("poolw", [P, DEPTH, 2, P])[0]
    poolcur = sb("poolcur", [P, 2, P])[0]
    parcur = sb("parcur", [P, 8])[0]
    gates = sb("gates", [P, 2, 24])[0]
    st = sb("st", [P, 4, 4, 4])[0]
    stc = sb("stc", [P, 4, 16])[0]
    KC = sb("KC", [P, 30])[0]
    VC = sb("VC", [16, 2, HD], at=low_at)[0]

    Y = sb("Y", [P, KD, S], at=hsB_at)[0]
    RH = sb("RH", [P, 2, 16, 60], F32R, at=hsB_at + 8192)[0]
    HC = sb("HC", [P, 2, 30], at=hsB_at + 8192 + 7680)[0]
    UB, _, ub_end = sb("UB", [P, 2, 2, S + 2], at=hsB_at)
    CB, _, cb_end = sb("CB", [P, 2, 2, S], at=ub_end)
    HB, _, hb_end = sb("HB", [P, 2, S], at=cb_end)
    assert hb_end <= hsB_end
    w = [ws_at]

    def ws(name, shape, dt=F32):
        h, _, w[0] = sb(name, shape, dt, at=w[0])
        assert w[0] <= ws_end, (name, w[0], ws_end)
        return h
    U1 = ws("U1", [P, 16, S])
    QR = ws("QR", [P, 4, S])
    KSW = ws("KSW", [P, 3, S])
    V1 = ws("V1", [P, 3, 2, P])
    PB = ws("PB", [P, 4, 512])
    PC = sb("PC", [P, 2, 8, 16], at=w[0])[0]
    PT = ws("PT", [P, 2, 512])
    w[0] = ws_at
    SG = ws("SG", [P, 4, S])
    TA = ws("TA", [P, 4, S])
    MX = ws("MX", [P, 2, S])
    MS = ws("MS", [P, KD, 2 * S], F32R)
    w[0] = ws_at
    U2 = ws("U2", [P, 20, S])
    V2 = ws("V2", [P, 2, 512])
    SPA = ws("SPA", [P, 2, 384])
    SPB = ws("SPB", [P, 2, 384])
    AB = ws("AB", [P, 2, 384])
    CU = ws("CU", [P, 2, S + 2])
    PS = ws("PS", [P, 5, S + 16])
    w[0] = ws_at
    rows = ws("rows", [P, 7, P])
    xin = ws("xin", [P, 2, D])
    posi = ws("posi", [P, S], I32)
    ang = ws("ang", [P, 6, S])
    w[0] = ws_at
    XO = ws("XO", [P, 2, D])
    assert top[0] <= nc.sbuf_usable_end, (top[0], nc.sbuf_usable_end)
    PCT = U1[0:16, 8:16, :].rearrange("p (n j) t -> p n (j t)", n=4)

    bank = [ctx.enter_context(nc.psum_tensor(f"bank{n}", [P, 512], F32)) for n in range(8)]

    def C(name):
        at, n = CONST_AT[name]
        return const[:, at:at + n]
    ident = C("ident")

    G1 = {"pre": 0, "post": 16, "fpre": 32, "fpost": 48}
    B1, PSC, CV2, NG2 = 64, 68, 72, 84

    def sem(name):
        return ctx.enter_context(nc.semaphore(name))

    landed = [sem(f"landed{n}") for n in range(RING)]
    whi_ready = sem("whi_ready")
    wlo_ready = sem("wlo_ready")
    params_in, consts_in, x_in = sem("params_in"), sem("consts_in"), sem("x_in")
    cleared, angles_ready, tables_ready = sem("cleared"), sem("angles_ready"), sem("tables_ready")
    rows_t, x_t, x_out = sem("rows_t"), sem("x_t"), sem("x_out")
    o_t, o_rows, out_done = sem("o_t"), sem("o_rows"), sem("out_done")
    awake = sem("awake")
    layer_end, layer_go = sem("layer_end"), sem("layer_go")
    stage_sems = []

    def lsem(name):
        stage_sems.append(sem(name))
        return stage_sems[-1]
    act_seq, dve_seq, pool_seq = lsem("act_seq"), lsem("dve_seq"), lsem("pool_seq")
    sum_ready = lsem("sum_ready")
    low_ready = lsem("low_ready")
    tile_out = lsem("tile_out")
    sq_ready, sq_used = lsem("sq_ready"), lsem("sq_used")
    rstd_ready = lsem("rstd_ready")
    x_ready, h_ready, hi_ready, hs_ready = lsem("x_ready"), lsem("h_ready"), lsem("hi_ready"), lsem("hs_ready")
    cur_ready = lsem("cur_ready")
    gates_sum, gates_ready = lsem("gates_sum"), lsem("gates_ready")
    swap_ready, swap_used = lsem("swap_ready"), lsem("swap_used")
    cosmul_ready, rope_done, kswap_done = lsem("cosmul_ready"), lsem("rope_done"), lsem("kswap_done")
    vt_ready, vt_out = lsem("vt_ready"), lsem("vt_out")
    cmp_in, cmp_hi, cmp_rhs, cmp_hid = lsem("cmp_in"), lsem("cmp_hi"), lsem("cmp_rhs"), lsem("cmp_hid")
    cmp_kv, cmp_kv_out = lsem("cmp_kv"), lsem("cmp_kv_out")
    cmp_z, cmp_x, cmp_e, cmp_p = lsem("cmp_z"), lsem("cmp_x"), lsem("cmp_e"), lsem("cmp_p")
    cmp_t, cmp_t_out = lsem("cmp_t"), lsem("cmp_t_out")
    scores_ready, nmax_ready, exp_ready, inv_ready = lsem("scores_ready"), lsem("nmax_ready"), lsem("exp_ready"), lsem("inv_ready")
    probs_ready, pt_ready, pt_out, pv_done = lsem("probs_ready"), lsem("pt_ready"), lsem("pt_out"), lsem("pv_done")
    o_hi, o_done = lsem("o_hi"), lsem("o_done")
    sg_ready, mix_ready, mix_hi, mix_split = lsem("sg_ready"), lsem("mix_ready"), lsem("mix_hi"), lsem("mix_split")
    c0_ready, conv_ready, act_ready = lsem("c0_ready"), lsem("conv_ready"), lsem("act_ready")
    hid_ready = lsem("hid_ready")
    z_ready, ln_ready, sp_ready = lsem("z_ready"), lsem("ln_ready"), lsem("sp_ready")
    cum_ready, ab_ready = lsem("cum_ready"), lsem("ab_ready")
    sc_ready, sc_hi, pool_in, pool_sum = lsem("sc_ready"), lsem("sc_hi"), lsem("pool_in"), lsem("pool_sum")

    block = ctx.enter_context(nc.Block())

    def first_chunk(blk, L):
        return L * CHUNKS_1 if blk == 1 else L * CHUNKS_2 + DEPTH * CHUNKS_1

    def landings(blk, L, c_div, slot):
        before = 0 if blk == 1 else DEPTH * PER_SLOT[1][slot]
        return L * (32 * PER_SLOT[blk][slot]) + c_div * 32 + (32 * before + 32)

    def o_places(o, p):
        g, qb, hs = UNITS[o % 6]
        r, j0, nj = HD * p, 4 * (o // 6) + hs[0] // 2, len(hs) // 2
        src = bank[2 + o % 2][0:HD, 0:len(hs) * P].rearrange("d (j e q) -> d j e q", e=2, q=P)[:, :, p, :]
        return (lambda part: hsB[r:r + HD, j0:j0 + nj, part * S + qb * P:part * S + qb * P + P]), src

    def score_place(i, x, keys):
        return bank[(0 if i % 2 else 4) + x % 2][:, x // 2 * keys:x // 2 * keys + keys]

    class Seq:

        def __init__(self, eng, s):
            self.eng, self.s, self.n, self.base = eng, s, 0, 0

        def link(self, ins):
            self.n += 1
            ins.then_inc(self.s, 1)
            self.eng.wait_ge(self.s, self.base + self.n)

        def restart(self, base):
            self.base, self.n = base, 0

    @block.sync
    def _(sp):
        def load(blk, L, c, slot, parts, lag=RING):
            sp.wait_ge(wlo_ready, 2 * (first_chunk(blk, L) + c) + (2 * (RING - lag) + 2))
            for dst, src in parts:
                sp.dma_start(dst, src).then_inc(landed[slot], 16)

        def pick(ap, L, c0, width, f=None):
            cs = slice(c0, c0 + width) if isinstance(c0, int) else ds(c0, width)
            if f is None:
                v = ap.rearrange("l (k p) n -> p l k n", p=P)[:, ds(L, 1), :, cs]
            else:
                v = ap.rearrange("l f (k p) n -> p l f k n", p=P)[:, ds(L, 1), f, :, cs]
            return v.rearrange("p a k n -> p (a k) n")

        def panel(blk, L, c, slot, ap, c0, **kw):
            v = pick(ap, L, c0, 256)
            d = raw[:, slot, :].rearrange("p (k n) -> p k n", n=256)
            load(blk, L, c, slot, [(d[:, x:x + 4], v[:, x:x + 4]) for x in (0, 4)], **kw)

        def two(blk, L, c, slot, views, **kw):
            d = raw[:, slot, :].rearrange("p (m k n) -> p m k n", m=2, n=P)
            load(blk, L, c, slot, [(d[:, m], v) for m, v in enumerate(views)], **kw)

        def down(blk, L, c0, ap, f=None):
            for n in range(16):
                slot, k0 = (c0 + n) % RING, (n % 2) * HALF_K
                v = pick(ap, L, n // 2 * P, P, f)
                d = raw[:, slot, 0:CH_DOWN].rearrange("p (k n) -> p k n", n=P)
                load(blk, L, c0 + n, slot, [(d[:, x:y], v[:, k0 + x:k0 + y]) for x, y in ((0, 6), (6, HALF_K))])

        with sp.Fori(0, DEPTH) as L:
            with sp.Fori(0, 2) as i:
                for s in range(4):
                    panel(1, L, i * 4 + s, s, a["w_in"], i * 1024 + s * 256)
            for n in range(2):
                v = a["cmp_w1"].rearrange("l t (k p) n -> p l t k n", p=P)[:, ds(L, 1), n].rearrange("p a k n -> p (a k) n")
                d = raw[:, n, :].rearrange("p (k n) -> p k n", n=P)
                load(1, L, C1["cmp"] + n, n, [(d[:, x:x + 8], v[:, x:x + 8]) for x in (0, 8)])
            for r in range(12):
                c = C1["branch"] + r
                q = r // 3
                if r % 3 < 2:
                    j = 2 * q + r % 3
                    two(1, L, c, c % RING, [pick(a["w_in"], L, GA_COL + b * D + j * P, P) for b in range(2)])
                else:
                    d = raw[:, c % RING, :].rearrange("p (b k n) -> p b k n", b=2, n=256)
                    load(1, L, c, c % RING, [(d[:, b], pick(a[nm], L, q * 256, 256))
                                             for b, nm in enumerate(("w_branch_a", "w_branch_b"))])
            for n in range(4):
                c = C1["out"] + n
                panel(1, L, c, c % RING, a["w_out"], n * 256)

            def up(c, slot, j):
                two(1, L, c, slot, [pick(a["ffn_w_up"], L, j + b * FF, P) for b in range(2)])
            c = C1["up"]
            with sp.Fori(0, 5) as i:
                for s in range(4):
                    up(i * 4 + (c + s), (c + s) % RING, i * 512 + s * P)
            for s in range(20, 22):
                up(c + s, (c + s) % RING, s * P)
            down(1, L, C1["down"], a["ffn_w_down"])

        with sp.Fori(0, DEPTH) as L:
            def ffn(f):
                c = C2[f"up{f}"]

                def pair(c, slot, j, lag=RING):
                    two(2, L, c, slot, [pick(a[nm], L, j, P, f) for nm in ("ffn_w_gate_2", "ffn_w_up_2")], lag=lag)
                for s in range(2):
                    pair(c + s, (c + s) % RING, s * P, lag=RING if f else 2)
                with sp.Fori(0, 5) as i:
                    for s in range(2, 6):
                        pair(i * 4 + (c + s), (c + s) % RING, i * 512 + s * P)
                down(2, L, C2[f"down{f}"], a["ffn_w_down_2"], f)

            ffn(0)
            c = C2["in"]
            with sp.Fori(0, 2) as i:
                for s in range(4):
                    panel(2, L, i * 4 + (c + s), (c + s) % RING, a["w_in_2"], i * 1024 + s * 256)
            for s in range(8, 10):
                panel(2, L, c + s, (c + s) % RING, a["w_in_2"], s * 256)
            for s in range(4):
                c = C2["out"] + s
                panel(2, L, c, c % RING, a["w_out_2"], s * 256)
            ffn(1)
        sp.wait_ge(o_rows, 4)
        sp.dma_start(out.rearrange("a (h p) n -> p (a h) n", p=P), XO[:, :, :]).then_inc(out_done, 16)
        sp.wait_ge(out_done, 16)

    @block.scalar
    def _(act):
        seq = Seq(act, act_seq)

        def f(out_, in_, func, **kw):
            if func == ACT.Copy:
                return nc.scalar.activation(out_, in_, func, **kw)
            kw.setdefault("bias", 0.0)
            kw.setdefault("scale", 1.0)
            return nc.scalar.activation(out_, in_, func, **kw)

        def split(blk, L, c_div, slot, size, part):
            if part == 0:
                act.wait_ge(landed[slot], landings(blk, L, c_div, slot))
            x, y = CUT[size][part]
            f(whi[slot][:, x:y], raw[:, slot, x:y], ACT.Copy).then_inc(whi_ready, 1)

        def split_at(blk, L, c):
            if c < len(SIZES[blk]):
                for part in range(2):
                    split(blk, L, c // RING, c % RING, SIZES[blk][c], part)

        def low_copy(t, b, n=S, scale=1.0):
            act.wait_ge(sum_ready, t + 1)
            f(low[:, b, 0:n], bank[b][:, n:2 * n], ACT.Copy, scale=scale).then_inc(low_ready, 1)

        def norm_stats(k):
            act.preload_act_table_set("natural_log_exp_and_others")
            act.wait_ge(sq_used, 8 * k)
            seq.link(f(rstd[:, :], bank[4][:, 0:S], ACT.Ln, bias=col[:, 0:1]))
            f(rstd[:, :], rstd[:, :], ACT.Exp, scale=-0.5).then_inc(rstd_ready, 1)

        def square(q, src):
            if q >= 2:
                act.wait_ge(sq_used, q - 1)
            f(sq[:, q % 2, :], src, ACT.Square).then_inc(sq_ready, 1)

        def norm_in(k, p):
            if k:
                norm_stats(k)
            for j in range(KD):
                act.wait_ge(h_ready, 8 * p + j + 1)
                f(hsA[:, j, 0:S], Y[:, j, :], ACT.Copy).then_inc(hi_ready, 1)

        def norm_out(k, p):
            norm_stats(k)
            for j in range(KD):
                act.wait_ge(x_ready, 8 * p + j + 1)
                square(8 * k + j, xT[:, j, :])

        def norm_next(k):
            norm_stats(k)

        def y_stage(blk, L, c0, t0, steps, set_):
            per = len(steps) // KD if len(steps) > KD else 1
            done = 0
            for n in range(len(steps)):
                split_at(blk, L, c0 + n + 2)
                for _ in range(steps[n]):
                    low_copy(t0 + done, (t0 + done) % 4)
                    if done:
                        act.wait_ge(tile_out, t0 + done + 4)
                        square(8 * set_ + done - 1, Y[:, done - 1, :])
                    done += 1
            act.wait_ge(tile_out, t0 + done + 4)
            square(8 * set_ + done - 1, Y[:, done - 1, :])

        DOWN, OUT = [0, 1] * 8, [2] * 4

        act.dma_start(const[:, :], a["const"]).then_inc(consts_in, 16)
        act.dma_start(posi[:, :], a["positions"][0:1, :].broadcast_to([P, S])).then_inc(consts_in, 16)
        for h in range(2):
            act.dma_start(xin[:, h, :], a["x"][0, h * P:(h + 1) * P, :]).then_inc(x_in, 16)

        def pin(dst, src):
            act.dma_start(dst, src).then_inc(params_in, 16)
        act.wait_ge(cleared, 1)
        for n, nm in enumerate(("attn_pre_gain", "attn_post_gain", "ffn_pre_gain", "ffn_post_gain")):
            pin(rows[16 * n:16 * n + 16, 0, :], a[nm].rearrange("l (j p) -> (l j) p", p=P))
        pin(rows[B1:B1 + 4, 0, :], a["cmp_b1"].rearrange("l t p -> (l t) p"))
        pin(rows[PSC:PSC + 4, 0, :], a["pool_scale_2"].rearrange("l (j p) -> (l j) p", p=P))
        pin(rows[CV2:CV2 + 12, 0, :], a["conv_w_2"].rearrange("l k (j p) -> (l k j) p", p=P))
        pin(rows[0:96, 1, :], a["norm_g_2"].rearrange("l g (j p) -> (l g j) p", p=P))
        for l in range(DEPTH):
            for k in range(3):
                pin(rows[44 * l:44 * l + 44, 2 + k, :], a["ffn_conv_w"][l, k].rearrange("(j p) -> j p", p=P))
            pin(rows[44 * l:44 * l + 44, 5, :], a["ffn_conv_b"][l].rearrange("(j p) -> j p", p=P))
        for h in range(2):
            pin(rows[:, 6, HD * h:HD * h + HD], a["cmp_pos_emb"].rearrange("l t c d -> (l t c) d"))
        pin(w2all[:, :, :, :], a["cmp_w2"].rearrange("l t p d -> p l t d"))
        for l in range(DEPTH):
            pin(wg[:, l, :, :], a["w_in"][l, :, GATE_COL:GA_COL].rearrange("(k p) n -> p k n", p=P))
            pin(sink[:, l, :], a["attn_sinks"][l:l + 1, :].broadcast_to([P, 8]))
            for g in range(4):
                r = HD * (g % 2)
                pin(poolw[r:r + HD, l, g // 2, r:r + HD], a["pool_w_2"][l, g])
        act.wait_ge(angles_ready, 1)
        f(sinT[:, :], ang[:, 3, :], ACT.Sin)
        f(cosT[:, :], ang[:, 4, :], ACT.Sin).then_inc(tables_ready, 1)
        for j in range(KD):
            act.wait_ge(x_out, j // 2 + 1)
            square(j, xT[:, j, :])
        norm_next(1)
        act.drain().then_inc(layer_end, 1)

        with act.Fori(0, DEPTH) as L:
            split_at(1, L, 0)
            act.wait_ge(layer_go, L + 1)
            act.sem_inc(awake, 1)
            seq.restart(0)
            for n in range(2):
                for h in range(2):
                    ins = f(w2cur[:, n, h, :], w2all[:, ds(L, 1), n, :].rearrange("p a d -> p (a d)"), ACT.Copy)
            ins.then_inc(cur_ready, 1)
            norm_in(0, 0)
            split_at(1, L, 1)
            for c in range(10):
                split_at(1, L, c + 2)
                if c in (7, 8):
                    n = c - 7
                    act.wait_ge(cmp_in, n + 1)
                    f(RH[:, n, :, 0:30], PB[:, n, 0:480].rearrange("p (k c) -> p k c", c=30), ACT.Copy).then_inc(cmp_hi, 1)
                if c < 8:
                    for t in (2 * c, 2 * c + 1):
                        low_copy(t, t % 4)
                else:
                    low_copy(T1["cmp"] + c - 8, (T1["cmp"] + c) % 4, n=30)
                if c == 1:
                    act.wait_ge(gates_sum, 1)
                    f(gates[:, :, :], bank[4][:, 0:48].rearrange("p (b n) -> p b n", n=24), ACT.Sigmoid).then_inc(gates_ready, 1)
                for n, (t, place) in enumerate(KEYS):
                    if t // 2 + 1 == c:
                        act.wait_ge(rope_done, ROPE.index(t) + 1)
                        f(KSW[HD:P, n, :], U1[0:HD, place, :], ACT.Copy)
                        f(KSW[0:HD, n, :], U1[HD:P, place, :], ACT.Copy).then_inc(kswap_done, 1)
                for n, t in enumerate(VALS):
                    if t // 2 + 1 == c:
                        act.wait_ge(vt_ready, n + 1)
                        f(V1[:, n, :, :], bank[6][:, 0:S].rearrange("p (b k) -> p b k", k=P), ACT.Copy).then_inc(vt_out, 1)
                if c >= 8:
                    n = c - 8
                    act.wait_ge(tile_out, T1["cmp"] + n + 5)
                    f(HC[:, n, :], HC[:, n, :], ACT.Gelu_apprx_tanh,
                      bias=gainT[:, ds(L * 2 + (B1 + n), 1)]).then_inc(cmp_hid, 1)
            act.wait_ge(cmp_kv, 1)
            f(KC[:, :], bank[6][:, 0:30], ACT.Copy)
            f(VC[0:N_CMP, :, :], bank[6][0:N_CMP, P:2 * P].rearrange("p (g d) -> p g d", g=2), ACT.Copy).then_inc(cmp_kv_out, 1)
            act.wait_ge(cmp_x, 1)
            f(PC[:, :, :, 0:N_CMP], PC[:, :, :, 0:N_CMP], ACT.Exp, scale=SCALE).then_inc(cmp_e, 1)
            for n in range(4):
                act.wait_ge(cmp_t, n + 1)
                f(PCT[0:N_CMP, n, :], bank[4 + n][0:N_CMP, :], ACT.Copy).then_inc(cmp_t_out, 1)

            for i in range(len(MAPS) + 5):
                if i < len(MAPS):
                    u, br = MAPS[i]
                    nh = len(UNITS[u][2])
                    keys = 512 // nh
                    s_ = st[:, i % 4]
                    act.wait_ge(nmax_ready, i + 1)
                    if br == 0:
                        f(s_[:, 2, 0:nh], s_[:, 2, 0:nh], ACT.Exp)
                    for x in range(nh):
                        p_ = PB[:, i % 4, x * keys:(x + 1) * keys]
                        ins = f(p_, p_, ACT.Exp, bias=s_[:, 0, x:x + 1], scale=SCALE, accum_out=s_[:, 1, x:x + 1])
                    ins.then_inc(exp_ready, 1)
                m = i - 2
                if 0 <= m < len(MAPS):
                    act.wait_ge(pt_ready, m + 1)
                    if m >= 2:
                        act.wait_ge(pv_done, m - 1)
                    f(PT[:, m % 2, :], bank[6 + m % 2][:, :], ACT.Copy).then_inc(pt_out, 1)
                m = i - 4
                if m in LAST_MAP:
                    o = LAST_MAP.index(m)
                    g, qb, hs = UNITS[o % 6]
                    act.wait_ge(pv_done, m + 1)
                    for p in range(2):
                        dst, src = o_places(o, p)
                        ins = f(dst(0), src, ACT.Copy)
                    ins.then_inc(o_hi, 1)

            for r in range(12):
                c, q = C1["branch"] + r, r // 3
                split_at(1, L, c + 2)
                t = T1["branch"] + 8 * q + (2 * (r % 3) if r % 3 < 2 else 4)
                for n in range(2 if r % 3 < 2 else 4):
                    low_copy(t + n, (t + n) % 4)
                if r % 3 < 2:
                    for n in range(2):
                        act.wait_ge(tile_out, t + n + 5)
                        k = (r % 3) * 2 + n
                        f(SG[:, k, :], SG[:, k, :], ACT.Sigmoid).then_inc(sg_ready, 1)
                else:
                    for m in range(2):
                        j = 2 * q + m
                        act.wait_ge(mix_ready, j + 1)
                        f(MS[:, j, 0:S], MX[:, m, :], ACT.Copy).then_inc(mix_hi, 1)
            y_stage(1, L, C1["out"], T1["out"], OUT, 0)
            norm_out(1, 0)
            norm_in(2, 1)

            def up(j, s, c_div, nslot, size):
                for n in range(2):
                    low_copy(2 * j + (T1["up"] + n), (T1["up"] + 2 * s + n) % 4)
                split(1, L, c_div, nslot, size, 0)
                for n in range(2):
                    act.wait_ge(tile_out, 2 * j + (T1["up"] + n + 5))
                    act.wait_ge(hid_ready, j + 1)
                    k = L * 44 + j + 22 * n
                    f(CB[:, s % 2, n, :], UB[:, s % 2, n, 2:S + 2], ACT.Identity,
                      scale=convT[:, 2, ds(k, 1)], bias=convT[:, 3, ds(k, 1)]).then_inc(c0_ready, 1)
                split(1, L, c_div, nslot, size, 1)
                act.wait_ge(conv_ready, 2 * j + 2)
                f(CB[:, s % 2, 0, :], CB[:, s % 2, 0, :], ACT.Gelu_apprx_tanh).then_inc(act_ready, 1)
            c = C1["up"]
            act.preload_act_table_set("gelu_apprx_tanh_and_others")
            with act.Fori(0, 5) as i:
                for s in range(4):
                    up(i * 4 + s, s, i + (c + s + 2) // RING, (c + s + 2) % RING, CH)
            for s in range(20, 22):
                up(s, s, (c + s + 2) // RING, (c + s + 2) % RING, CH_DOWN)
            y_stage(1, L, C1["down"], T1["down"], DOWN, 2)
            norm_out(3, 1)
            norm_next(4)
            act.drain().then_inc(layer_end, 1)

        with act.Fori(0, DEPTH) as L:
            split_at(2, L, 0)
            act.wait_ge(layer_go, L + (DEPTH + 1))
            act.sem_inc(awake, 1)
            seq.restart(0)
            f(parcur[:, 0:6], gainT[:, ds(L * 6 + CV2, 6)], ACT.Copy)
            f(parcur[:, 6:8], gainT[:, ds(L * 2 + PSC, 2)], ACT.Copy)
            f(poolcur[:, :, :], poolw[:, ds(L, 1), :, :].rearrange("p a n d -> p (a n) d"), ACT.Copy).then_inc(cur_ready, 1)

            def ffn(n_ffn):
                c, t0 = C2[f"up{n_ffn}"], T2[f"up{n_ffn}"]

                def pair(j, s, c_div, nslot, size):
                    for n in range(2):
                        low_copy(2 * j + (t0 + n), (t0 + 2 * s + n) % 4)
                    split(2, L, c_div, nslot, size, 0)
                    act.wait_ge(tile_out, 2 * j + (t0 + 5))
                    act.wait_ge(hid_ready, j + (22 * n_ffn + 1))
                    f(CB[:, s % 2, 0, :], UB[:, s % 2, 0, 2:S + 2], ACT.Silu).then_inc(act_ready, 1)
                    split(2, L, c_div, nslot, size, 1)
                act.preload_act_table_set("silu_and_others")
                with act.Fori(0, 5) as i:
                    for s in range(4):
                        pair(i * 4 + s, s, i + (c + s + 2) // RING, (c + s + 2) % RING, CH)
                for s in range(20, 22):
                    pair(s, s, (c + s + 2) // RING, (c + s + 2) % RING, CH_DOWN)
                y_stage(2, L, C2[f"down{n_ffn}"], T2[f"down{n_ffn}"], DOWN, 4 * n_ffn)

            norm_in(0, 0)
            split_at(2, L, 1)
            ffn(0)
            norm_out(1, 0)
            norm_in(2, 1)
            for n in range(10):
                split_at(2, L, C2["in"] + n + 2)
                for t in (2 * n, 2 * n + 1):
                    low_copy(T2["in"] + t, (T2["in"] + t) % 4, scale=SCALE if t < 4 else 1.0)
                for q in range(4):
                    if (8 + q) // 2 + 1 == n:
                        act.wait_ge(vt_ready, q + 1)
                        f(V2[:, :, q * P:(q + 1) * P], bank[6 + q % 2][:, 0:S].rearrange("p (b k) -> p b k", k=P), ACT.Copy)\
                            .then_inc(vt_out, 1)
            act.preload_act_table_set("natural_log_exp_and_others")
            for i in range(8 + 3):
                if i < 8:
                    act.wait_ge(z_ready, i + 1)
                    if i >= 2:
                        act.wait_ge(sp_ready, i - 1)
                    s_ = SPA[:, i % 2, :]
                    seq.link(f(s_, bank[4 + i % 2][:, 0:384], ACT.Abs))
                    seq.link(f(s_, s_, ACT.Exp, scale=-1.0))
                    f(s_, s_, ACT.Ln, bias=col[:, 1:2]).then_inc(ln_ready, 1)
                h = i - 1
                if 0 <= h < 8:
                    act.wait_ge(cum_ready, h + 1)
                    if h >= 2:
                        act.wait_ge(pv_done, h - 1)
                    f(AB[:, h % 2, :], bank[4 + h % 2][:, 0:384], ACT.Exp).then_inc(ab_ready, 1)
                h = i - 3
                if 0 <= h < 8:
                    act.wait_ge(pv_done, h + 1)
                    r = HD * (h % 2)
                    f(hsA[r:r + HD, h // 2, 0:S], bank[6 + h % 2][0:HD, 0:S], ACT.Copy).then_inc(o_hi, 1)
            for n in range(2):
                act.wait_ge(sc_ready, n + 1)
                f(hsA[:, 4 + n, 0:S], U2[:, 12 + n, :], ACT.Copy).then_inc(sc_hi, 1)
            for n in range(2):
                act.wait_ge(pool_sum, n + 1)
                f(hsA[:, 6 + n, 0:S], bank[n][:, 0:S], ACT.Copy, scale=parcur[:, 6 + n:7 + n]).then_inc(sc_hi, 1)
            y_stage(2, L, C2["out"], T2["out"], OUT, 2)
            norm_out(3, 1)
            norm_in(4, 2)
            ffn(1)
            norm_out(5, 2)
            norm_next(6)
            act.drain().then_inc(layer_end, 1)

        for n in range(2):
            act.wait_ge(o_t, n + 1)
            f(XO[:, n // 2, n % 2 * 512:n % 2 * 512 + 512], bank[n][:, :], ACT.Copy).then_inc(o_rows, 1)

    @block.vector
    def _(dve):
        seq = Seq(dve, dve_seq)
        v = nc.vector

        def split(blk, L, c, slot, size, part):
            dve.wait_ge(whi_ready, 2 * (first_chunk(blk, L) + c) + (part + 1))
            x, y = CUT[size][part]
            v.tensor_tensor(wlo[slot][:, x:y], raw[:, slot, x:y], whi[slot][:, x:y].bitcast(F32), ALU.subtract)\
                .then_inc(wlo_ready, 1)

        def split_at(blk, L, c):
            if c < len(SIZES[blk]):
                for part in range(2):
                    split(blk, L, c, c % RING, SIZES[blk][c], part)

        def tile_sum(t, b, dst, n=S, scale=1.0):
            dve.wait_ge(low_ready, t + 1)
            if scale == 1.0:
                v.tensor_tensor(dst, bank[b][:, 0:n], low[:, b, 0:n], ALU.add).then_inc(tile_out, 1)
            else:
                v.scalar_tensor_tensor(dst, bank[b][:, 0:n], scale, low[:, b, 0:n], ALU.mult, ALU.add).then_inc(tile_out, 1)

        def norm_in(k, p, gain):
            if k:
                dve.wait_ge(rstd_ready, k)

            def lo(j):
                dve.wait_ge(hi_ready, 8 * p + j + 1)
                v.tensor_tensor(hsA[:, j, S:2 * S], Y[:, j, :], hsA[:, j, 0:S].bitcast(F32), ALU.subtract).then_inc(hs_ready, 1)
            for j in range(KD):
                v.scalar_tensor_tensor(Y[:, j, :], xT[:, j, :], gainT[:, ds(gain + j, 1)], rstd[:, :],
                                       ALU.mult, ALU.mult).then_inc(h_ready, 1)
                if j:
                    lo(j - 1)
            lo(KD - 1)
            dve.wait_ge(hs_ready, 8 * p + 8)

        def norm_out(k, p, gain):
            dve.wait_ge(tile_out_now[0], tile_out_now[1])
            dve.wait_ge(rstd_ready, k)
            for j in range(KD):
                seq.link(v.scalar_tensor_tensor(tm[:, j % 2, :], Y[:, j, :], gainT[:, ds(gain + j, 1)], rstd[:, :],
                                                ALU.mult, ALU.mult))
                v.tensor_tensor(xT[:, j, :], xT[:, j, :], tm[:, j % 2, :], ALU.add).then_inc(x_ready, 1)
            dve.wait_ge(x_ready, 8 * p + 8)

        def y_stage(blk, L, c0, t0, steps):
            done = 0
            for n in range(len(steps)):
                split_at(blk, L, c0 + n + 2)
                for _ in range(steps[n]):
                    tile_sum(t0 + done, (t0 + done) % 4, Y[:, done, :])
                    done += 1
            tile_out_now[:] = [tile_out, t0 + done + 4]

        tile_out_now = [None, 0]
        DOWN, OUT = [0, 1] * 8, [2] * 4

        def end_layer(n):
            dve.wait_ge(layer_end, n * 3)
            dve.sem_inc(awake, 1)
            dve.drain()
            dve.sem_clear(range(stage_sems[0].num, stage_sems[-1].num + 1))
            dve.sem_inc(tile_out, 4)
            dve.sem_inc(hid_ready, 2)
            dve.sem_inc(layer_go, 1)
            dve.wait_ge(layer_go, n)

        dve.sem_inc(wlo_ready, 2 * RING)
        v.memset(poolw[:, :, :, :], 0.0)
        v.memset(mean_w[:, :], 1.0 / D)
        v.memset(nones[:, :], -1.0)
        v.memset(col[:, 0:1], EPS)
        v.memset(col[:, 1:2], 1.0)
        v.memset(rows[:, :, :], 0.0).then_inc(cleared, 1)
        dve.wait_ge(consts_in, 32)
        seq.link(v.tensor_copy(ang[:, 0, :], posi[:, :]))
        seq.link(v.tensor_scalar(ang[:, 0, :], ang[:, 0, :], C("freq"), None, ALU.mult))
        for n, turn in ((3, 0.0), (4, 0.25)):
            k, r = ang[:, 1, :], ang[:, n, :]
            seq.link(v.tensor_scalar(k, ang[:, 0, :], 1.0 / TWO_PI, turn, ALU.mult, ALU.add))
            seq.link(v.tensor_scalar(k, k, ROUND, None, ALU.add))
            seq.link(v.tensor_scalar(k, k, ROUND, None, ALU.subtract))
            seq.link(v.scalar_tensor_tensor(r, k, -PI_A, ang[:, 0, :], ALU.mult, ALU.add))
            seq.link(v.scalar_tensor_tensor(r, k, -PI_B, r, ALU.mult, ALU.add))
            seq.link(v.scalar_tensor_tensor(r, k, -PI_C, r, ALU.mult, ALU.add))
            seq.link(v.tensor_scalar(r, r, turn * TWO_PI, PI_MAX, ALU.add, ALU.min))
            seq.link(v.tensor_scalar(r, r, -PI_MAX, None, ALU.max))
        dve.sem_inc(angles_ready, 1)
        for n in range(4):
            dve.wait_ge(x_t, n + 1)
            v.tensor_copy(xT[:, 2 * n:2 * n + 2, :], bank[4 + n][:, :].rearrange("p (j t) -> p j t", j=2)).then_inc(x_out, 1)
        dve.wait_ge(rows_t, 1)
        v.tensor_copy(gainT[:, 0:NG2], bank[0][:, 0:NG2])
        v.tensor_copy(gainT[:, NG2:NG2 + 96], bank[0][:, P:P + 96])
        for k in range(2):
            v.tensor_copy(convT[:, k, :], bank[0][:, (2 + k) * P:(2 + k) * P + 88])
            v.tensor_copy(convT[:, 2 + k, :], bank[1][:, k * P:k * P + 88])
        seq.link(v.tensor_copy(posT[:, :], bank[1][:, 2 * P:3 * P]))
        for l in range(DEPTH):
            for g in (1, 5):
                at = NG2 + l * 48 + g * 8
                seq.link(v.tensor_scalar(gainT[:, at:at + 8], gainT[:, at:at + 8], 0.5, None, ALU.mult))
        dve.wait_ge(params_in, 16 * N_PARAMS)
        seq.link(v.tensor_scalar(nsink[:, :, :], sink[:, :, :], -1.0, None, ALU.mult))
        dve.wait_ge(tables_ready, 1)
        seq.link(v.tensor_scalar(sinT[:, :], sinT[:, :], C("sign"), None, ALU.mult))
        end_layer(1)

        with dve.Fori(0, DEPTH) as L:
            seq.restart(0)
            split_at(1, L, 0)
            norm_in(0, 0, L * 8 + G1["pre"])
            split_at(1, L, 1)

            def rope(r):
                t = ROPE[r]
                dst = U1[:, PLACE[t], :] if t < 6 or t > 9 else QR[:, t - 6, :]
                dve.wait_ge(swap_ready, r + 1)
                v.tensor_tensor(tm[:, r % 2, :], bank[5 + 2 * (r % 2)][:, 0:S], sinT[:, :], ALU.mult).then_inc(swap_used, 1)
                dve.wait_ge(swap_used, r + 1)
                dve.wait_ge(cosmul_ready, r + 1)
                v.tensor_tensor(dst, sq[:, r % 2, :], tm[:, r % 2, :], ALU.add).then_inc(rope_done, 1)

            def cmp_build(n):
                dve.wait_ge(tile_out, T1["in"] + 10 + n + 5)
                dst = PB[:, n, 0:480].rearrange("p (k g c) -> p k g c", g=2, c=N_CMP)
                pos = posT[:, ds(L * 64 + n * 32, 32)].rearrange("p (k e) -> p k e", e=2)
                for g in range(2):
                    src = U1[HD * g:HD * g + HD, KCB + n, :].rearrange("p (c l) -> p l c", l=16)
                    for par in range(2):
                        for h in range(2):
                            ins = v.tensor_tensor(
                                dst[HD * par:HD * par + HD, 8 * h:8 * h + 8, g, :],
                                src[:, par:16:2, h:h + N_CMP],
                                pos[HD * g:HD * g + HD, 8 * h:8 * h + 8, par:par + 1].broadcast_to([HD, 8, N_CMP]), ALU.add)
                ins.then_inc(cmp_in, 1)

            def cmp_lo(n):
                dve.wait_ge(cmp_hi, n + 1)
                v.tensor_tensor(RH[:, n, :, 30:60], PB[:, n, 0:480].rearrange("p (k c) -> p k c", c=30),
                                RH[:, n, :, 0:30].bitcast(F32), ALU.subtract).then_inc(cmp_rhs, 1)

            for c in range(10):
                split_at(1, L, c + 2)
                if c in (7, 8):
                    cmp_lo(c - 7)
                if c < 8:
                    for t in (2 * c, 2 * c + 1):
                        tile_sum(t, t % 4, U1[:, PLACE[t], :])
                else:
                    t = T1["cmp"] + c - 8
                    tile_sum(t, t % 4, HC[:, c - 8, :], n=30)
                for r, t in enumerate(ROPE):
                    if t // 2 + 1 == c:
                        rope(r)
                if c in (6, 7):
                    cmp_build(c - 6)
            dve.wait_ge(gates_ready, 1)
            dve.wait_ge(cmp_z, 1)
            z = [bank[7 - 2 * par][:, 0:P].rearrange("p (b h c) -> p b h c", b=2, h=4) for par in range(2)]
            mask = C("mask_cmp").rearrange("p (b c) -> p b c", b=2)
            for qb in range(2):
                for par in range(2):
                    ins = v.tensor_tensor(PC[:, qb, par:8:2, 0:N_CMP], z[par][:, qb, :, 0:N_CMP],
                                          mask[:, qb:qb + 1, 0:N_CMP].broadcast_to([P, 4, N_CMP]), ALU.add)
            seq.link(ins)
            rowsP = PC[:, :, :, 0:N_CMP].rearrange("p b h c -> p (b h) c")

            def per_row(k):
                return stc[:, k, :].unsqueeze(2).broadcast_to([P, 16, N_CMP])
            seq.link(v.tensor_reduce(stc[:, 0, :], rowsP, AX_X, ALU.max))
            seq.link(v.tensor_scalar(stc[:, 0, :], stc[:, 0, :], 0.1 * NEG, None, ALU.max))
            v.tensor_tensor(rowsP, rowsP, per_row(0), ALU.subtract).then_inc(cmp_x, 1)
            dve.wait_ge(cmp_e, 1)
            seq.link(v.tensor_reduce(stc[:, 1, :], rowsP, AX_X, ALU.add))
            seq.link(v.tensor_scalar(stc[:, 1, :], stc[:, 1, :], TINY, None, ALU.max))
            seq.link(v.reciprocal(stc[:, 2, :], stc[:, 1, :]))
            gate = gates[:, :, :].rearrange("p b (h n) -> p (b h) n", n=3)
            seq.link(v.tensor_tensor(stc[:, 3, :], stc[:, 2, :], gate[:, :, 0], ALU.mult))
            v.tensor_tensor(rowsP, rowsP, per_row(3), ALU.mult).then_inc(cmp_p, 1)

            for i in range(len(MAPS) + 5):
                if i < len(MAPS):
                    u, br = MAPS[i]
                    g, qb, hs = UNITS[u]
                    nh = len(hs)
                    keys = 512 // nh
                    s_ = st[:, i % 4]
                    m_ = C("mask_c" if br else "mask_a")[:, (1 - qb) * P:2 * P]
                    dve.wait_ge(scores_ready, i + 1)
                    if i >= 4:
                        dve.wait_ge(pt_ready, i - 3)
                    for x in range(nh):
                        ins = v.tensor_tensor_reduce(PB[:, i % 4, x * keys:(x + 1) * keys], score_place(i, x, keys),
                                                     m_, 1.0, 3 * NEG, ALU.add, ALU.max, s_[:, 0, x:x + 1])
                    seq.link(ins)
                    if br:
                        v.tensor_scalar(s_[:, 0, 0:nh], s_[:, 0, 0:nh], -SCALE, None, ALU.mult).then_inc(nmax_ready, 1)
                    else:
                        hd = slice(hs[0], hs[0] + nh)
                        seq.link(v.scalar_tensor_tensor(s_[:, 0, 0:nh], s_[:, 0, 0:nh], -SCALE,
                                                        nsink[:, ds(L, 1), hd].rearrange("p a h -> p (a h)"), ALU.mult, ALU.min))
                        v.tensor_tensor(s_[:, 2, 0:nh], s_[:, 0, 0:nh], sink[:, ds(L, 1), hd].rearrange("p a h -> p (a h)"),
                                        ALU.add).then_inc(nmax_ready, 1)
                m = i - 1
                if 0 <= m < len(MAPS):
                    u, br = MAPS[m]
                    g, qb, hs = UNITS[u]
                    nh = len(hs)
                    s_ = st[:, m % 4]
                    dve.wait_ge(exp_ready, m + 1)
                    if br:
                        seq.link(v.tensor_scalar(s_[:, 1, 0:nh], s_[:, 1, 0:nh], TINY, None, ALU.max))
                        seq.link(v.reciprocal(s_[:, 2, 0:nh], s_[:, 1, 0:nh]))
                        v.tensor_tensor(s_[:, 3, 0:nh], s_[:, 2, 0:nh],
                                        gate[:, 8 * qb + hs[0]:8 * qb + hs[0] + nh, br], ALU.mult).then_inc(inv_ready, 1)
                    else:
                        seq.link(v.tensor_tensor(s_[:, 1, 0:nh], s_[:, 1, 0:nh], s_[:, 2, 0:nh], ALU.add))
                        v.reciprocal(s_[:, 3, 0:nh], s_[:, 1, 0:nh]).then_inc(inv_ready, 1)
                m = i - 4
                if m in LAST_MAP:
                    o = LAST_MAP.index(m)
                    dve.wait_ge(o_hi, o + 1)
                    for p in range(2):
                        dst, src = o_places(o, p)
                        ins = v.tensor_tensor(dst(1), src, dst(0).bitcast(F32), ALU.subtract)
                    ins.then_inc(o_done, 1)

            for r in range(12):
                c, q = C1["branch"] + r, r // 3
                split_at(1, L, c + 2)
                t = T1["branch"] + 8 * q + (2 * (r % 3) if r % 3 < 2 else 4)
                if q:
                    dve.wait_ge(mix_ready, 2 * q)
                for n in range(2 if r % 3 < 2 else 4):
                    tile_sum(t + n, (t + n) % 4, SG[:, (r % 3) * 2 + n, :] if r % 3 < 2 else TA[:, n, :])
                if r % 3 == 2:
                    for m in range(2):
                        j = 2 * q + m
                        dve.wait_ge(mix_hi, j + 1)
                        v.tensor_tensor(MS[:, j, S:2 * S], MX[:, m, :], MS[:, j, 0:S].bitcast(F32), ALU.subtract).then_inc(mix_split, 1)
            y_stage(1, L, C1["out"], T1["out"], OUT)
            norm_out(1, 0, L * 8 + G1["post"])
            norm_in(2, 1, L * 8 + G1["fpre"])

            seq.link(v.memset(UB[:, :, :, 0:2], 0.0))

            def up(j, s, c, nslot, size, pre):
                for n in range(2):
                    tile_sum(2 * j + (T1["up"] + n), (T1["up"] + 2 * s + n) % 4, UB[:, s % 2, n, 2:S + 2])
                split(1, L, c, nslot, size, 0)
                for n in range(2):
                    k = L * 44 + j + 22 * n
                    y = CB[:, s % 2, n, :]
                    dve.wait_ge(c0_ready, 2 * j + (n + 1))
                    seq.link(v.scalar_tensor_tensor(y, UB[:, s % 2, n, 1:S + 1], convT[:, 1, ds(k, 1)], y, ALU.mult, ALU.add))
                    v.scalar_tensor_tensor(y, UB[:, s % 2, n, 0:S], convT[:, 0, ds(k, 1)], y, ALU.mult, ALU.add).then_inc(conv_ready, 1)
                split(1, L, c, nslot, size, 1)
                dve.wait_ge(wlo_ready, 2 * (first_chunk(1, L) + c) + (2 * RING + 2))
            c = C1["up"]
            kept = seq.n
            with dve.Fori(0, 5) as i:
                seq.restart(kept + i * 8)
                for s in range(4):
                    up(i * 4 + s, s, i * 4 + (c + s + 2), (c + s + 2) % RING, CH, None)
                assert seq.n == 8
            seq.restart(0)
            seq.n = kept + 40
            for s in range(20, 22):
                up(s, s, c + s + 2, (c + s + 2) % RING, CH_DOWN, None)
            y_stage(1, L, C1["down"], T1["down"], DOWN)
            norm_out(3, 1, L * 8 + G1["fpost"])
            end_layer(L + 2)

        with dve.Fori(0, DEPTH) as L:
            seq.restart(0)
            split_at(2, L, 0)

            def gain(g):
                return L * 48 + (NG2 + 8 * g)

            def ffn(n_ffn):
                c, t0 = C2[f"up{n_ffn}"], T2[f"up{n_ffn}"]

                def pair(j, s, cc, nslot, size):
                    dve.wait_ge(hid_ready, j + (22 * n_ffn + 1))
                    for n in range(2):
                        tile_sum(2 * j + (t0 + n), (t0 + 2 * s + n) % 4, UB[:, s % 2, n, 2:S + 2])
                    split(2, L, cc, nslot, size, 0)
                    split(2, L, cc, nslot, size, 1)
                with dve.Fori(0, 5) as i:
                    for s in range(4):
                        pair(i * 4 + s, s, i * 4 + (c + s + 2), (c + s + 2) % RING, CH)
                for s in range(20, 22):
                    pair(s, s, c + s + 2, (c + s + 2) % RING, CH_DOWN)
                y_stage(2, L, C2[f"down{n_ffn}"], T2[f"down{n_ffn}"], DOWN)

            norm_in(0, 0, gain(0))
            split_at(2, L, 1)
            ffn(0)
            norm_out(1, 0, gain(1))
            norm_in(2, 1, gain(2))
            for n in range(10):
                split_at(2, L, C2["in"] + n + 2)
                for t in (2 * n, 2 * n + 1):
                    tile_sum(T2["in"] + t, (T2["in"] + t) % 4, U2[:, t, :], scale=SCALE if t < 4 else 1.0)
            for i in range(8 + 3):
                h = i
                if 0 <= h < 8:
                    dve.wait_ge(ln_ready, h + 1)
                    v.scalar_tensor_tensor(SPB[:, h % 2, :], bank[4 + h % 2][:, 0:384], 0.0, SPA[:, h % 2, :],
                                           ALU.max, ALU.add).then_inc(sp_ready, 1)
                h = i - 3
                if 0 <= h < 8:
                    dve.wait_ge(o_hi, h + 1)
                    r = HD * (h % 2)
                    v.tensor_tensor(hsA[r:r + HD, h // 2, S:2 * S], bank[6 + h % 2][0:HD, 0:S],
                                    hsA[r:r + HD, h // 2, 0:S].bitcast(F32), ALU.subtract).then_inc(o_done, 1)
            for n in range(2):
                dve.wait_ge(sc_hi, n + 1)
                v.tensor_tensor(hsA[:, 4 + n, S:2 * S], U2[:, 12 + n, :], hsA[:, 4 + n, 0:S].bitcast(F32), ALU.subtract).then_inc(o_done, 1)
            for n in range(2):
                dve.wait_ge(sc_hi, n + 3)
                v.scalar_tensor_tensor(hsA[:, 6 + n, S:2 * S], bank[n][:, 0:S], parcur[:, 6 + n:7 + n],
                                       hsA[:, 6 + n, 0:S].bitcast(F32), ALU.mult, ALU.subtract).then_inc(o_done, 1)
            y_stage(2, L, C2["out"], T2["out"], OUT)
            norm_out(3, 1, gain(3))
            norm_in(4, 2, gain(4))
            ffn(1)
            norm_out(5, 2, gain(5))
            end_layer(L + 4)

        for n in range(2, 4):
            dve.wait_ge(o_t, n + 1)
            v.tensor_copy(XO[:, n // 2, n % 2 * 512:n % 2 * 512 + 512], bank[n][:, :]).then_inc(o_rows, 1)

    @block.gpsimd
    def _(pool):
        seq = Seq(pool, pool_seq)
        g_ = nc.gpsimd

        def squares(set_):
            if set_:
                pool.wait_ge(sq_used, 8 * set_)
            for j in range(1, KD - 1):
                q = 8 * set_ + j
                pool.wait_ge(sq_ready, q + 1)
                g_.tensor_tensor(sqsum[:, :], sq[:, 0, :] if j == 1 else sqsum[:, :], sq[:, q % 2, :], ALU.add)\
                    .then_inc(sq_used, 2 if j == 1 else 1)
                pool.wait_ge(sq_used, q + 1)

        def product(j, s, other, n0, t0=None):
            pool.wait_ge(hid_ready, j + (22 * n0 + 2))
            pool.wait_ge(act_ready, j + (22 * n0 + 1))
            if t0 is not None:
                pool.wait_ge(tile_out, 2 * j + (t0 + 1 + 5))
            x, y = CB[:, s % 2, 0, :], other
            dst = hid[:, ds(j, 1), :].rearrange("p a t -> p (a t)") if not isinstance(j, int) else hid[:, j, :]
            g_.tensor_tensor(HB[:, s % 2, :], x, y, ALU.mult)
            seq.link(g_.tensor_tensor(dst[:, 0:S], x, y, ALU.mult))
            g_.tensor_tensor(dst[:, S:2 * S], HB[:, s % 2, :], dst[:, 0:S].bitcast(F32), ALU.subtract).then_inc(hid_ready, 1)

        pool.drain().then_inc(layer_end, 1)
        with pool.Fori(0, DEPTH) as L:
            pool.wait_ge(layer_go, L + 1)
            pool.sem_inc(awake, 1)
            seq.restart(0)
            for r, t in enumerate(ROPE):
                pool.wait_ge(tile_out, T1["in"] + t + 5)
                if r >= 2:
                    pool.wait_ge(rope_done, r - 1)
                g_.tensor_tensor(sq[:, r % 2, :], U1[:, PLACE[t], :], cosT[:, :], ALU.mult).then_inc(cosmul_ready, 1)
            for m, (u, br) in enumerate(MAPS):
                nh = len(UNITS[u][2])
                keys = 512 // nh
                pool.wait_ge(inv_ready, m + 1)
                for x in range(nh):
                    p_ = PB[:, m % 4, x * keys:(x + 1) * keys]
                    ins = g_.tensor_scalar(p_, p_, st[:, m % 4, 3, x:x + 1], 1.0, ALU.mult, ALU.mult)
                ins.then_inc(probs_ready, 1)
            for j in range(KD):
                q, m = j // 2, j % 2
                pool.wait_ge(sg_ready, 4 * q + 2 * m + 2)
                pool.wait_ge(tile_out, T1["branch"] + 8 * q + 4 + 2 * m + 2 + 4)
                g_.tensor_tensor(TA[:, 2 * m, :], TA[:, 2 * m, :], SG[:, 2 * m, :], ALU.mult)
                seq.link(g_.tensor_tensor(TA[:, 2 * m + 1, :], TA[:, 2 * m + 1, :], SG[:, 2 * m + 1, :], ALU.mult))
                if j >= 2:
                    pool.wait_ge(mix_split, j - 1)
                g_.tensor_tensor(MX[:, m, :], TA[:, 2 * m, :], TA[:, 2 * m + 1, :], ALU.add).then_inc(mix_ready, 1)
                pool.wait_ge(mix_ready, j + 1)
            squares(0)
            kept = seq.n
            with pool.Fori(0, 5) as i:
                seq.restart(kept + i * 4)
                for s in range(4):
                    product(i * 4 + s, s, CB[:, s % 2, 1, :], 0)
            seq.restart(0)
            seq.n = kept + 20
            for s in range(20, 22):
                product(s, s, CB[:, s % 2, 1, :], 0)
            pool.wait_ge(hid_ready, KF + 2)
            squares(2)
            pool.drain().then_inc(layer_end, 1)

        with pool.Fori(0, DEPTH) as L:
            pool.wait_ge(layer_go, L + (DEPTH + 1))
            pool.sem_inc(awake, 1)
            seq.restart(0)

            def ffn(n_ffn):
                kept = seq.n
                with pool.Fori(0, 5) as i:
                    seq.restart(kept + i * 4)
                    for s in range(4):
                        product(i * 4 + s, s, UB[:, s % 2, 1, 2:S + 2], n_ffn, T2[f"up{n_ffn}"])
                seq.restart(0)
                seq.n = kept + 20
                for s in range(20, 22):
                    product(s, s, UB[:, s % 2, 1, 2:S + 2], n_ffn, T2[f"up{n_ffn}"])
                pool.wait_ge(hid_ready, KF * (n_ffn + 1) + 2)
                squares(4 * n_ffn)
            ffn(0)
            pool.wait_ge(cur_ready, 1)
            pool.wait_ge(tile_out, T2["in"] + 20 + 4)
            seq.link(g_.memset(CU[:, :, 0:2], 0.0))
            seq.link(g_.memset(PS[:, :, 0:16], 0.0))
            for n in range(2):
                gb, y, t = U2[:, 12 + n, :], U2[:, 14 + n, :], U2[:, 16 + n, :]

                def tap(k):
                    return parcur[:, 2 * k + n:2 * k + n + 1]
                seq.link(g_.tensor_tensor(CU[:, n, 2:S + 2], y, t, ALU.mult))
                g_.tensor_scalar(y, CU[:, n, 0:S], tap(0), 1.0, ALU.mult, ALU.mult)
                seq.link(g_.tensor_scalar(t, CU[:, n, 1:S + 1], tap(1), 1.0, ALU.mult, ALU.mult))
                seq.link(g_.tensor_tensor(y, y, t, ALU.add))
                seq.link(g_.tensor_scalar(t, CU[:, n, 2:S + 2], tap(2), 1.0, ALU.mult, ALU.mult))
                seq.link(g_.tensor_tensor(y, y, t, ALU.add))
                g_.tensor_tensor(gb, gb, y, ALU.mult).then_inc(sc_ready, 1)
                pool.wait_ge(sc_ready, n + 1)
            for n in range(2):
                p_ = U2[:, 18 + n, :]
                src = p_
                seq.link(g_.tensor_copy(PS[:, 0, 16:], p_))
                for k in range(2 + 2 * n):
                    w_ = 1 << k
                    seq.link(g_.tensor_tensor(PS[:, k + 1, 16:], PS[:, k, 16:], PS[:, k, 16 - w_:16 + S - w_], ALU.add))
                d = PS[:, 0, 16:]
                cnt = C("count").rearrange("p (n c) -> p n c", n=2)
                for half in range(2):
                    rr = slice(HD * half, HD * half + HD)
                    sm = PS[rr, 1 + 2 * n + half, 16:]
                    seq.link(g_.tensor_scalar(d[rr, :], sm, C("width")[rr, n:n + 1], 1.0, ALU.mult, ALU.mult))
                    seq.link(g_.tensor_tensor(d[rr, 0:16], sm[:, 0:16], cnt[rr, n, :], ALU.mult))
                g_.tensor_tensor(p_, d, p_, ALU.subtract).then_inc(pool_in, 1)
                pool.wait_ge(pool_in, n + 1)
            squares(2)
            ffn(1)
            pool.drain().then_inc(layer_end, 1)

    @block.tensor
    def _(pe):
        mm = nc.tensor.matmul
        g32 = dict(skip_group_check=True)

        def chunk_here(blk, L, c):
            pe.wait_ge(wlo_ready, 2 * (first_chunk(blk, L) + c) + (2 * RING + 2))

        def tile(t, b, slot, ks, first=True, last=True, n=S):
            if first:
                pe.wait_ge(tile_out, t + 1)
            for x, (at, rhs, wait) in enumerate(ks):
                if wait:
                    pe.wait_ge(*wait)
                end = last and x == len(ks) - 1
                mm(bank[b][:, 0:2 * n], whi[slot][:, at:at + P], rhs[:, 0:2 * n], start=first and x == 0, stop=False, **g32)
                ins = mm(bank[b][:, n:2 * n], wlo[slot][:, at:at + P], rhs[:, 0:n], start=False, stop=end, **g32)
            if last:
                ins.then_inc(sum_ready, 1)

        def norm_post(k):
            pe.wait_ge(sq_used, 8 * k + 7)
            mm(bank[4][:, 0:S], mean_w[:, :], sqsum[:, :], start=True, stop=False, **g32)
            pe.wait_ge(sq_ready, 8 * k + 8)
            mm(bank[4][:, 0:S], mean_w[:, :], sq[:, 1, :], start=False, stop=True, **g32).then_inc(sq_used, 1)

        def norm_pre(k):
            for j in range(KD):
                pe.wait_ge(sq_ready, 8 * k + j + 1)
                mm(bank[4][:, 0:S], mean_w[:, :], sq[:, j % 2, :], start=j == 0, stop=j == KD - 1, **g32).then_inc(sq_used, 1)

        def hs_waits(p):
            return [(hs_ready, 8 * p + k + 1) for k in range(KD)]

        def panel(t, b, slot, rhs):
            for m in range(2):
                tile(t + m, (b + m) % 4, slot, [(k * 256 + m * P, rhs[:, k, :], None) for k in range(KD)])

        def pair(t, b, slot, rhs):
            for m in range(2):
                tile(t + m, (b + m) % 4, slot, [((m * KD + k) * P, rhs[:, k, :], None) for k in range(KD)])

        def both(t, slot, at, rhs, waits):
            pe.wait_ge(tile_out, t + 2)
            for k in range(KD):
                pe.wait_ge(*waits[k])
                for m in range(2):
                    b = (t + m) % 4
                    mm(bank[b][:, 0:2 * S], whi[slot][:, at(m, k):at(m, k) + P], rhs[:, k, :], start=k == 0, stop=False, **g32)
                    ins = mm(bank[b][:, S:2 * S], wlo[slot][:, at(m, k):at(m, k) + P], rhs[:, k, 0:S],
                             start=False, stop=k == KD - 1, **g32)
                    if k == KD - 1:
                        ins.then_inc(sum_ready, 1)

        def in_panel(m, k):
            return k * 256 + m * P

        def in_pair(m, k):
            return (m * KD + k) * P

        def down(blk, L, c0, t0, wait):
            pe.wait_ge(*wait)
            for n in range(16):
                c, t = c0 + n, t0 + n // 2
                chunk_here(blk, L, c)
                tile(t, t % 4, c % RING, [(k * P, hid[:, n % 2 * HALF_K + k, :], None) for k in range(HALF_K)],
                     first=n % 2 == 0, last=n % 2 == 1)

        def up_pairs(blk, L, c, t, waits):
            chunk_here(blk, L, c)
            both(t, c % RING, in_pair, hsA, waits)
            with pe.Fori(0, 5) as i:
                for s in range(1, 5):
                    chunk_here(blk, L, i * 4 + (c + s))
                    pair(i * 8 + (t + 2 * s), (t + 2 * s) % 4, (c + s) % RING, hsA)
            chunk_here(blk, L, c + 21)
            pair(t + 42, (t + 42) % 4, (c + 21) % RING, hsA)

        pe.wait_ge(consts_in, 32)
        pe.wait_ge(x_in, 32)
        for n in range(4):
            for j in range(2):
                for h in range(2):
                    ins = nc.tensor.transpose(bank[4 + n][:, j * S + h * P:j * S + h * P + P],
                                              xin[:, h, (2 * n + j) * P:(2 * n + j + 1) * P], ident)
            ins.then_inc(x_t, 1)
        pe.wait_ge(params_in, 16 * N_PARAMS)
        for r in range(7):
            ins = nc.tensor.transpose(bank[r // 4][:, r % 4 * P:r % 4 * P + P], rows[:, r, :], ident)
        ins.then_inc(rows_t, 1)
        pe.wait_ge(cleared, 1)
        norm_pre(0)
        pe.drain().then_inc(layer_end, 1)

        with pe.Fori(0, DEPTH) as L:
            pe.wait_ge(layer_go, L + 1)
            pe.sem_inc(awake, 1)
            for c in range(8):
                chunk_here(1, L, c)
                if c == 0:
                    both(0, 0, in_panel, hsA, hs_waits(0))
                else:
                    panel(2 * c, 2 * c, c % RING, hsA)
                if c == 0:
                    for b in range(2):
                        for k in range(KD):
                            ins = mm(bank[4][:, 24 * b:24 * b + 24], Y[:, k, b * P:(b + 1) * P],
                                     wg[:, ds(L, 1), k, :].rearrange("p a n -> p (a n)"),
                                     start=k == 0, stop=k == KD - 1, **g32)
                    ins.then_inc(gates_sum, 1)
                for cc in ([c - 1] if c < 7 else [6, 7]):
                    for t in (2 * cc, 2 * cc + 1):
                        if t in ROPE:
                            r = ROPE.index(t)
                            pe.wait_ge(tile_out, T1["in"] + t + 5)
                            if r >= 2:
                                pe.wait_ge(swap_used, r - 1)
                            mm(bank[5 + 2 * (r % 2)][:, 0:S], C("swap"), U1[:, PLACE[t], :], start=True, stop=True, **g32)\
                                .then_inc(swap_ready, 1)
                        if t in VALS:
                            n = VALS.index(t)
                            pe.wait_ge(tile_out, T1["in"] + t + 5)
                            if n:
                                pe.wait_ge(vt_out, n)
                            for b in range(2):
                                ins = nc.tensor.transpose(bank[6][:, b * P:b * P + P], U1[:, PLACE[t], b * P:b * P + P], ident)
                            ins.then_inc(vt_ready, 1)
            pe.wait_ge(cur_ready, 1)
            for n in range(2):
                c, t = C1["cmp"] + n, T1["cmp"] + n
                chunk_here(1, L, c)
                pe.wait_ge(cmp_rhs, n + 1)
                tile(t, t % 4, c % RING, [(k * P, RH[:, n, k, :], None) for k in range(16)], n=30)
            pe.wait_ge(cmp_hid, 2)
            pe.wait_ge(vt_out, 3)
            mm(bank[6][:, 0:30], w2cur[:, 0, :, :].rearrange("p r d -> p (r d)"), HC[:, 0, :], start=True, stop=True, **g32)
            for g in range(2):
                ins = mm(bank[6][0:N_CMP, P + HD * g:P + HD * g + HD], HC[:, 1, N_CMP * g:N_CMP * g + N_CMP], w2cur[:, 1, 0, :],
                         start=True, stop=True, **g32)
            ins.then_inc(cmp_kv, 1)
            pe.wait_ge(cmp_kv_out, 1)
            pe.wait_ge(rope_done, len(ROPE))
            for qb in range(2):
                for h in range(8):
                    r, at = HD * (h % 2), (4 * qb + h // 2) * 16
                    ins = mm(bank[7 - 2 * (h % 2)][:, at:at + N_CMP], U1[r:r + HD, QB + h // 2, qb * P:qb * P + P],
                             KC[r:r + HD, N_CMP * (h // 4):N_CMP * (h // 4) + N_CMP], start=True, stop=True, **g32)
            ins.then_inc(cmp_z, 1)
            pe.wait_ge(cmp_p, 1)
            for n in range(4):
                g, qb = n // 2, n % 2
                for x in range(4):
                    ins = nc.tensor.transpose(bank[4 + n][0:N_CMP, x * P:(x + 1) * P], PC[:, qb, 4 * g + x, 0:N_CMP], ident)
                ins.then_inc(cmp_t, 1)

            pe.wait_ge(kswap_done, 3)
            pe.wait_ge(cmp_t_out, 4)
            pe.wait_ge(tile_out, T1["cmp"] + 2 + 4)
            for i in range(len(MAPS) + 3):
                if i < len(MAPS):
                    u, br = MAPS[i]
                    g, qb, hs = UNITS[u]
                    keys = 512 // len(hs)
                    if i >= 2:
                        pe.wait_ge(nmax_ready, i - 1)
                    for x, h in enumerate(hs):
                        r = HD * (h % 2)
                        q_ = (QR if br else U1)[r:r + HD, h // 2, qb * P:qb * P + P]
                        k_ = (U1[r:r + HD, (KA, KS, KW)[br], 0:keys] if h % 2 == g else KSW[r:r + HD, br, 0:keys])
                        ins = mm(score_place(i, x, keys), q_, k_, start=True, stop=True, **g32)
                    ins.then_inc(scores_ready, 1)
                m = i - 2
                if 0 <= m < len(MAPS):
                    nh = len(UNITS[MAPS[m][0]][2])
                    nk = 4 // nh
                    pe.wait_ge(probs_ready, m + 1)
                    if m >= 2:
                        pe.wait_ge(pt_out, m - 1)
                    for kb in range(nk):
                        for x in range(nh):
                            ins = nc.tensor.transpose(bank[6 + m % 2][:, (kb * nh + x) * P:(kb * nh + x + 1) * P],
                                                      PB[:, m % 4, (x * nk + kb) * P:(x * nk + kb + 1) * P], ident)
                    ins.then_inc(pt_ready, 1)
                m = i - 3
                if 0 <= m < len(MAPS):
                    u, br = MAPS[m]
                    g, qb, hs = UNITS[u]
                    nh = len(hs)
                    n = nh * P
                    o = m if br == 0 else 6 + u
                    O = bank[2 + o % 2][0:HD, 0:n]
                    pe.wait_ge(pt_out, m + 1)
                    if br < 2 and o >= 2:
                        pe.wait_ge(o_done, o - 1)
                    if br == 1:
                        x0 = (hs[0] - 4 * g) * P
                        mm(O, VC[0:N_CMP, g, :], PCT[0:N_CMP, 2 * g + qb, x0:x0 + n], start=True, stop=False, **g32)
                    for kb in range(qb + 1):
                        ins = mm(O, V1[:, br, kb, HD * g:HD * g + HD], PT[:, m % 2, kb * n:kb * n + n],
                                 start=br == 0 and kb == 0, stop=br != 1 and kb == qb, **g32)
                    ins.then_inc(pv_done, 1)

            pe.wait_ge(o_done, 12)
            for r in range(12):
                c, q = C1["branch"] + r, r // 3
                chunk_here(1, L, c)
                t = T1["branch"] + 8 * q + (2 * (r % 3) if r % 3 < 2 else 4)
                if r % 3 < 2:
                    pair(t, t % 4, c % RING, hsA)
                else:
                    for m in range(2):
                        for b in range(2):
                            tt = t + 2 * m + b
                            tile(tt, tt % 4, c % RING, [((4 * b + k) * 256 + m * P, hsB[:, 4 * b + k, :], None) for k in range(4)])
            for n in range(4):
                c, t = C1["out"] + n, T1["out"] + 2 * n
                chunk_here(1, L, c)
                if n == 0:
                    both(t, c % RING, in_panel, MS, [(mix_split, k + 1) for k in range(KD)])
                else:
                    panel(t, t % 4, c % RING, MS)
            norm_post(0)
            norm_pre(1)
            up_pairs(1, L, C1["up"], T1["up"], hs_waits(1))
            down(1, L, C1["down"], T1["down"], (hid_ready, KF + 2))
            norm_post(2)
            norm_pre(3)
            pe.drain().then_inc(layer_end, 1)

        with pe.Fori(0, DEPTH) as L:
            pe.wait_ge(layer_go, L + (DEPTH + 1))
            pe.sem_inc(awake, 1)

            def ffn(f, p):
                up_pairs(2, L, C2[f"up{f}"], T2[f"up{f}"], hs_waits(p))
                down(2, L, C2[f"down{f}"], T2[f"down{f}"], (hid_ready, KF * (f + 1) + 2))
            ffn(0, 0)
            norm_post(0)
            norm_pre(1)
            for n in range(10):
                c, t = C2["in"] + n, T2["in"] + 2 * n
                chunk_here(2, L, c)
                if n == 0:
                    both(t, c % RING, in_panel, hsA, hs_waits(1))
                else:
                    panel(t, t % 4, c % RING, hsA)
                for q in range(4):
                    if (8 + q) // 2 + 1 == n:
                        pe.wait_ge(tile_out, T2["in"] + 8 + q + 5)
                        if q >= 2:
                            pe.wait_ge(vt_out, q - 1)
                        for b in range(2):
                            ins = nc.tensor.transpose(bank[6 + q % 2][:, b * P:b * P + P], U2[:, 8 + q, b * P:b * P + P], ident)
                        ins.then_inc(vt_ready, 1)
            pe.wait_ge(vt_out, 4)
            stick = C("stick")
            for i in range(8 + 2):
                if i < 8:
                    r = HD * (i % 2)
                    q_, k_ = U2[r:r + HD, i // 2, :], U2[r:r + HD, 4 + i // 2, :]
                    b_ = bank[4 + i % 2]
                    if i >= 2:
                        pe.wait_ge(ab_ready, i - 1)
                    mm(b_[:, 0:S], k_[:, 0:P], q_, start=True, stop=False, **g32)
                    mm(b_[:, S:S + P], k_[:, P:S], q_[:, P:S], start=False, stop=False, **g32)
                    mm(b_[:, 0:P], ident, stick, start=False, stop=False, **g32)
                    mm(b_[:, S:S + P], ident, stick, start=False, stop=False, **g32).then_inc(z_ready, 1)
                h = i - 1
                if 0 <= h < 8:
                    b_, s_ = bank[4 + h % 2], SPB[:, h % 2, :]
                    pe.wait_ge(sp_ready, h + 1)
                    mm(b_[:, 0:S], C("ntri"), s_[:, 0:S], start=False, stop=False, **g32)
                    mm(b_[:, S:S + P], C("ntri"), s_[:, S:S + P], start=False, stop=False, **g32)
                    mm(b_[:, P:S], nones[:, :], s_[:, S:S + P], start=False, stop=True, **g32).then_inc(cum_ready, 1)
                h = i - 2
                if 0 <= h < 8:
                    pe.wait_ge(ab_ready, h + 1)
                    if h >= 2:
                        pe.wait_ge(o_done, h - 1)
                    b_ = bank[6 + h % 2]
                    mm(b_[0:HD, 0:S], V2[:, 0, h * HD:h * HD + HD], AB[:, h % 2, 0:S], start=True, stop=False, **g32)
                    mm(b_[0:HD, P:S], V2[:, 1, h * HD:h * HD + HD], AB[:, h % 2, S:S + P], start=False, stop=True, **g32)\
                        .then_inc(pv_done, 1)
            pe.wait_ge(tile_out, T2["in"] + 20 + 4)
            for n in range(2):
                pe.wait_ge(pool_in, n + 1)
                mm(bank[n][:, 0:S], poolcur[:, n, :], U2[:, 18 + n, :], start=True, stop=True, **g32).then_inc(pool_sum, 1)
            pe.wait_ge(o_done, 12)
            for n in range(4):
                c, t = C2["out"] + n, T2["out"] + 2 * n
                chunk_here(2, L, c)
                panel(t, t % 4, c % RING, hsA)
            norm_post(2)
            norm_pre(3)
            ffn(1, 2)
            norm_post(4)
            norm_pre(5)
            pe.drain().then_inc(layer_end, 1)

        pe.wait_ge(layer_go, 2 * DEPTH + 1)
        for n in range(4):
            for j in range(4):
                k = 4 * (n % 2) + j
                ins = nc.tensor.transpose(bank[n][:, j * P:(j + 1) * P], xT[:, k, n // 2 * P:n // 2 * P + P], ident)
            ins.then_inc(o_t, 1)

    ctx.close()


N_PARAMS = 4 + 4 + 8 + 2 + 1 + 2 * 6
INPUTS = ["x", "positions", "attn_pre_gain", "attn_post_gain", "ffn_pre_gain", "ffn_post_gain", "w_in", "attn_sinks",
          "cmp_pos_emb", "cmp_w1", "cmp_b1", "cmp_w2", "w_branch_a", "w_branch_b", "w_out", "ffn_w_up", "ffn_conv_w",
          "ffn_conv_b", "ffn_w_down", "norm_g_2", "ffn_w_gate_2", "ffn_w_up_2", "ffn_w_down_2", "w_in_2", "conv_w_2",
          "pool_w_2", "pool_scale_2", "w_out_2"]


def kernel(**inputs):
    from concourse import bacc
    from concourse.bass_utils import run_bass_kernel_spmd

    nc = bacc.Bacc("TRN2", target_bir_lowering=False, num_devices=1)
    arrays = {n: np.ascontiguousarray(inputs[n]) for n in INPUTS}
    arrays["const"] = host_constants()
    handles = {n: nc.dram_tensor(f"in_{n}", v.shape, mybir.dt.from_np(v.dtype), kind="ExternalInput").ap()
               for n, v in arrays.items()}
    out = nc.dram_tensor("result", (1, S, D), F32, kind="ExternalOutput").ap()
    build(nc, handles, out)
    got = run_bass_kernel_spmd(nc, [{f"in_{n}": v for n, v in arrays.items()}], core_ids=[0])
    return got.results[0]["result"]
```

```python
from contextlib import ExitStack

import numpy as np

import concourse.bass as bass
from concourse import mybir

F32 = mybir.dt.float32
F32R = mybir.dt.float32r
I32 = mybir.dt.int32
ALU = mybir.AluOpType
ACT = mybir.ActivationFunctionType
AX_X = mybir.AxisListType.X
ds = bass.ds

P = 128
S = 256
D = 1024
KD = D // P
DEPTH = 2
FF = 2816
KF = FF // P
HD = 64
EPS = 1e-6
TINY = 1e-30
NEG = -1e30
SCALE = HD ** -0.5
GATE_COL = 2048
GA_COL = GATE_COL + 24
N_CMP = 15
HALF_K = KF // 2
CH = 2048
CH_DOWN = HALF_K * P
RING = 4
TWO_PI = 2.0 * np.pi
PI_A = 6.28125
PI_B = float(np.float32(np.round((TWO_PI - PI_A) * 2.0 ** 20) / 2.0 ** 20))
PI_C = float(np.float32(TWO_PI - PI_A - PI_B))
ROUND = 12582912.0
PI_MAX = 3.1415925

CHUNKS_1 = 8 + 2 + 8 + 4 + 4 + 22 + 16
CHUNKS_2 = 22 + 16 + 10 + 4 + 22 + 16

CONST = {"ident": 128, "swap": 128, "ntri": 128, "stick": 128, "mask_a": 256, "mask_c": 256,
         "mask_cmp": 32, "count": 32, "width": 2, "freq": 1, "sign": 1}
CONST_AT, _n = {}, 0
for _k, _w in CONST.items():
    CONST_AT[_k] = (_n, _w)
    _n += _w
CONST_COLS = _n


def host_constants():
    c = np.zeros((P, CONST_COLS), np.float32)

    def put(name, a):
        at, w = CONST_AT[name]
        c[:, at:at + w] = np.asarray(a, np.float32).reshape(P, w)
    i = np.arange(P)
    put("ident", np.eye(P))
    put("swap", (i[:, None] == (i ^ 32)[None, :]))
    put("ntri", np.where(i[:, None] >= i[None, :], -1.0, 0.0))
    put("stick", np.where(i[:, None] < i[None, :], 0.0, NEG))
    tri = np.where(i[None, :] <= i[:, None], 0.0, NEG)
    put("mask_a", np.concatenate([np.where(i[None, :] > i[:, None], 0.0, NEG), tri], 1))
    put("mask_c", np.concatenate([np.zeros((P, P)), tri], 1))
    end = np.arange(16) * 16 + 31
    end[15] = 1 << 20
    t = np.stack([i, i + P], 1)
    put("mask_cmp", np.where(end[None, None, :] <= t[:, :, None], 0.0, NEG))
    width = np.where(i[:, None] < 64, [[2, 8]], [[4, 16]])
    put("count", 1.0 / np.minimum(np.arange(1, 17)[None, None, :], width[:, :, None]))
    put("width", 1.0 / width)
    put("freq", np.float32(10000.0) ** (-(i % 32).astype(np.float32) / np.float32(32)))
    put("sign", np.where(i % 64 < 32, -1.0, 1.0))
    return c


T1 = {"in": 0, "cmp": 18, "branch": 24, "out": 50, "up": 58, "down": 102}
T2 = {"up0": 0, "down0": 44, "in": 52, "out": 72, "up1": 80, "down1": 124}
C1 = {"in": 0, "cmp": 9, "branch": 13, "out": 22, "up": 26, "down": 48}
C2 = {"up0": 0, "down0": 22, "in": 38, "out": 48, "up1": 52, "down1": 74}
PER_SLOT = {1: [CHUNKS_1 // RING] * RING, 2: [(CHUNKS_2 + RING - 1 - n) // RING for n in range(RING)]}
SIZES = {1: [CH] * C1["down"] + [CH_DOWN] * 16,
         2: [CH] * 22 + [CH_DOWN] * 16 + [CH] * 36 + [CH_DOWN] * 16}
CUT = {CH: ((0, CH // 2), (CH // 2, CH)), CH_DOWN: ((0, 6 * P), (6 * P, CH_DOWN))}

EARLY = [(0, 8, 16), (1, 11, 20), (2, 12, 22)]
BRANCH, _t = [], T1["branch"]
for _kind, _x in (("mix", 0), ("gate", 3), ("mix", 1), ("gate", 4), ("gate", 5), ("mix", 2), ("gate", 6), ("gate", 7), ("mix", 3)):
    BRANCH.append((_kind, _x, C1["branch"] + len(BRANCH), _t))
    _t += 4 if _kind == "mix" else 2
assert _t == T1["out"] and BRANCH[-1][2] + 1 == C1["out"]
MIX_TILE = [t for kind, x, c, t in BRANCH if kind == "mix"]
SKEW = 3

DOWN_ORDER = [(0, 0), (1, 0), (0, 1), (1, 1)] + [(j, half) for j in range(2, KD) for half in range(2)]

QA, KA, KS, KW, VW, QB, KCB, VCB, VA, VS = 0, 4, 5, 6, 7, 8, 12, 13, 14, 15
PLACE = [QA, QA + 1, QA + 2, QA + 3, KA, VA, QB, QB + 1, QB + 2, QB + 3, KCB, VCB, KS, VS, KW, VW]
ROPE = [0, 1, 2, 3, 4, 6, 7, 8, 9, 12, 14]
VALS = [5, 13, 15]
KEYS = [(4, KA), (12, KS), (14, KW)]

UNITS = [(g, qb, hs) for g in range(2) for qb, hs in
         ((0, [4 * g + r for r in range(4)]), (1, [4 * g, 4 * g + 1]), (1, [4 * g + 2, 4 * g + 3]))]
OUT_GROUPS = [(0, 1), (1, 2), (2, 4), (4, 6), (6, 7), (7, 8)]
IN_GROUPS = [(0, 1), (1, 2), (2, 3), (3, 4), (4, 6), (6, 8)]
MAPS = [(u, 0) for u in range(6)] + [(u, b) for u in range(6) for b in (1, 2)]
LAST_MAP = list(range(6)) + [7 + 2 * u for u in range(6)]


def build(nc, a, out):
    ctx = ExitStack()
    top = [(nc.sbuf_base + 31) // 32 * 32]

    def sb(name, shape, dt=F32, at=None):
        size = (int(np.prod(shape[1:])) * 4 + 31) // 32 * 32
        if at is None:
            at = top[0]
            top[0] += size
        return nc.alloc_sbuf_tensor_at(name, list(shape), dt, offset=at), at, at + size

    raw = sb("raw", [P, RING, CH])[0]
    whi = [sb(f"whi{n}", [P, CH], F32R)[0] for n in range(RING)]
    wlo = [sb(f"wlo{n}", [P, CH], F32R)[0] for n in range(RING)]
    hsA = sb("hsA", [P, KD, 2 * S], F32R)[0]
    hsB, hsB_at, hsB_end = sb("hsB", [P, KD, 2 * S], F32R)
    hid, ws_at, ws_end = sb("hid", [P, KF, 2 * S], F32R)
    xT = sb("xT", [P, KD, S])[0]
    low, low_at, _ = sb("low", [P, 4, S])
    sq = sb("sq", [P, 2, S])[0]
    sqsum = sb("sqsum", [P, S])[0]
    rstd = sb("rstd", [P, S])[0]
    tm = sb("tm", [P, 2, S])[0]
    cosT = sb("cosT", [P, S])[0]
    sinT = sb("sinT", [P, S])[0]
    const = sb("const", [P, CONST_COLS])[0]
    mean_w = sb("mean_w", [P, P])[0]
    nones = sb("nones", [P, P])[0]
    col = sb("col", [P, 2])[0]
    gainT = sb("gainT", [P, 180])[0]
    convT = sb("convT", [P, 4, 88])[0]
    posT = sb("posT", [P, P])[0]
    w2all = sb("w2all", [P, DEPTH, 2, HD])[0]
    w2cur = sb("w2cur", [P, 2, 2, HD])[0]
    wg = sb("wg", [P, DEPTH, KD, 24])[0]
    sink = sb("sink", [P, DEPTH, 8])[0]
    nsink = sb("nsink", [P, DEPTH, 8])[0]
    poolw = sb("poolw", [P, DEPTH, 2, P])[0]
    poolcur = sb("poolcur", [P, 2, P])[0]
    parcur = sb("parcur", [P, 8])[0]
    gates = sb("gates", [P, 2, 24])[0]
    st = sb("st", [P, 4, 4, 4])[0]
    stc = sb("stc", [P, 4, 16])[0]
    KC = sb("KC", [P, 30])[0]
    VC = sb("VC", [16, 2, HD], at=low_at)[0]

    Y = sb("Y", [P, KD, S], at=hsB_at)[0]
    RH = sb("RH", [P, 2, 16, 60], F32R, at=hsB_at + 8192)[0]
    HC = sb("HC", [P, 2, 30], at=hsB_at + 8192 + 7680)[0]
    UB, _, ub_end = sb("UB", [P, 2, 2, S + 2], at=hsB_at)
    CB, _, cb_end = sb("CB", [P, 2, 2, S], at=ub_end)
    HB, _, hb_end = sb("HB", [P, 2, S], at=cb_end)
    assert hb_end <= hsB_end
    w = [ws_at]

    def ws(name, shape, dt=F32):
        h, _, w[0] = sb(name, shape, dt, at=w[0])
        assert w[0] <= ws_end, (name, w[0], ws_end)
        return h
    U1 = ws("U1", [P, 16, S])
    QR = ws("QR", [P, 4, S])
    KSW = ws("KSW", [P, 3, S])
    V1 = ws("V1", [P, 3, 2, P])
    PB = ws("PB", [P, 4, 512])
    PC = sb("PC", [P, 2, 8, 16], at=w[0])[0]
    PT = ws("PT", [P, 2, 512])
    SGE = ws("SGE", [P, 6, S])
    w[0] = ws_at
    SG = ws("SG", [P, 4, S])
    TA = ws("TA", [P, 4, S])
    MX = ws("MX", [P, 2, S])
    MS = ws("MS", [P, KD, 2 * S], F32R)
    w[0] = ws_at
    U2 = ws("U2", [P, 20, S])
    V2 = ws("V2", [P, 2, 512])
    SPA = ws("SPA", [P, 2, 384])
    SPB = ws("SPB", [P, 2, 384])
    AB = ws("AB", [P, 2, 384])
    CU = ws("CU", [P, 2, S + 2])
    PS = ws("PS", [P, 5, S + 16])
    w[0] = ws_at
    rows = ws("rows", [P, 7, P])
    xin = ws("xin", [P, 2, D])
    posi = ws("posi", [P, S], I32)
    ang = ws("ang", [P, 6, S])
    w[0] = ws_at
    XO = ws("XO", [P, 2, D])
    assert top[0] <= nc.sbuf_usable_end, (top[0], nc.sbuf_usable_end)
    PCT = U1[0:16, 8:16, :].rearrange("p (n j) t -> p n (j t)", n=4)

    bank = [ctx.enter_context(nc.psum_tensor(f"bank{n}", [P, 512], F32)) for n in range(8)]

    def C(name):
        at, n = CONST_AT[name]
        return const[:, at:at + n]
    ident = C("ident")

    G1 = {"pre": 0, "post": 16, "fpre": 32, "fpost": 48}
    B1, PSC, CV2, NG2 = 64, 68, 72, 84

    def sem(name):
        return ctx.enter_context(nc.semaphore(name))

    landed = [sem(f"landed{n}") for n in range(RING)]
    whi_ready = sem("whi_ready")
    wlo_ready = sem("wlo_ready")
    rows_in, params_in, consts_in, x_in = sem("rows_in"), sem("params_in"), sem("consts_in"), sem("x_in")
    cleared, angles_ready, tables_ready = sem("cleared"), sem("angles_ready"), sem("tables_ready")
    rows_t, x_t, x_out = sem("rows_t"), sem("x_t"), sem("x_out")
    o_t, o_rows, out_done = sem("o_t"), sem("o_rows"), sem("out_done")
    awake = sem("awake")
    layer_end, layer_go = sem("layer_end"), sem("layer_go")
    stage_sems = []

    def lsem(name):
        stage_sems.append(sem(name))
        return stage_sems[-1]
    act_seq, dve_seq, pool_seq = lsem("act_seq"), lsem("dve_seq"), lsem("pool_seq")
    sum_ready = lsem("sum_ready")
    low_ready = lsem("low_ready")
    tile_out = lsem("tile_out")
    sq_ready, sq_used = lsem("sq_ready"), lsem("sq_used")
    rstd_ready = lsem("rstd_ready")
    yg_ready = lsem("yg_ready")
    x_ready, h_ready, hi_ready, hs_ready = lsem("x_ready"), lsem("h_ready"), lsem("hi_ready"), lsem("hs_ready")
    cur_ready = lsem("cur_ready")
    gates_sum, gates_ready = lsem("gates_sum"), lsem("gates_ready")
    swap_ready, swap_used = lsem("swap_ready"), lsem("swap_used")
    cosmul_ready, rope_done, kswap_done = lsem("cosmul_ready"), lsem("rope_done"), lsem("kswap_done")
    vt_ready, vt_out = lsem("vt_ready"), lsem("vt_out")
    cmp_in, cmp_hi, cmp_rhs, cmp_hid = lsem("cmp_in"), lsem("cmp_hi"), lsem("cmp_rhs"), lsem("cmp_hid")
    cmp_kv, cmp_kv_out = lsem("cmp_kv"), lsem("cmp_kv_out")
    cmp_z, cmp_x, cmp_e, cmp_p = lsem("cmp_z"), lsem("cmp_x"), lsem("cmp_e"), lsem("cmp_p")
    cmp_t, cmp_t_out = lsem("cmp_t"), lsem("cmp_t_out")
    scores_ready, nmax_ready, exp_ready, inv_ready = lsem("scores_ready"), lsem("nmax_ready"), lsem("exp_ready"), lsem("inv_ready")
    probs_ready, pt_ready, pt_out, pv_done = lsem("probs_ready"), lsem("pt_ready"), lsem("pt_out"), lsem("pv_done")
    o_hi, o_done = lsem("o_hi"), lsem("o_done")
    sg_ready, mix_ready, mix_hi, mix_split = lsem("sg_ready"), lsem("mix_ready"), lsem("mix_hi"), lsem("mix_split")
    c0_ready, conv_ready, act_ready = lsem("c0_ready"), lsem("conv_ready"), lsem("act_ready")
    hid_ready = lsem("hid_ready")
    z_ready, ln_ready, sp_ready = lsem("z_ready"), lsem("ln_ready"), lsem("sp_ready")
    cum_ready, ab_ready = lsem("cum_ready"), lsem("ab_ready")
    sc_ready, sc_hi, pool_in, pool_sum = lsem("sc_ready"), lsem("sc_hi"), lsem("pool_in"), lsem("pool_sum")

    block = ctx.enter_context(nc.Block())

    def first_chunk(blk, L):
        return L * CHUNKS_1 if blk == 1 else L * CHUNKS_2 + DEPTH * CHUNKS_1

    def landings(blk, L, c_div, slot):
        before = 0 if blk == 1 else DEPTH * PER_SLOT[1][slot]
        return L * (32 * PER_SLOT[blk][slot]) + c_div * 32 + (32 * before + 32)

    def gate_place(j):
        return SGE[:, 2 * j:2 * j + 2, :] if j < len(EARLY) else SG[:, 2 * (j % 2):2 * (j % 2) + 2, :]

    def o_places(o, p):
        g, qb, hs = UNITS[o % 6]
        r, j0, nj = HD * p, 4 * (o // 6) + hs[0] // 2, len(hs) // 2
        src = bank[2 + o % 2][0:HD, 0:len(hs) * P].rearrange("d (j e q) -> d j e q", e=2, q=P)[:, :, p, :]
        return (lambda part: hsB[r:r + HD, j0:j0 + nj, part * S + qb * P:part * S + qb * P + P]), src

    def score_place(i, x, keys):
        return bank[(0 if i % 2 else 4) + x % 2][:, x // 2 * keys:x // 2 * keys + keys]

    def z_bank(h):
        return bank[(4, 5, 2, 3)[h % 4]]

    class Seq:

        def __init__(self, eng, s):
            self.eng, self.s, self.n, self.base = eng, s, 0, 0

        def link(self, ins):
            self.n += 1
            ins.then_inc(self.s, 1)
            self.eng.wait_ge(self.s, self.base + self.n)

        def restart(self, base):
            self.base, self.n = base, 0

    @block.sync
    def _(sp):
        def load(blk, L, c, slot, parts, lag=RING):
            sp.wait_ge(wlo_ready, 2 * (first_chunk(blk, L) + c) + (2 * (RING - lag) + 2))
            for dst, src in parts:
                sp.dma_start(dst, src).then_inc(landed[slot], 16)

        def pick(ap, L, c0, width, f=None):
            cs = slice(c0, c0 + width) if isinstance(c0, int) else ds(c0, width)
            if f is None:
                v = ap.rearrange("l (k p) n -> p l k n", p=P)[:, ds(L, 1), :, cs]
            else:
                v = ap.rearrange("l f (k p) n -> p l f k n", p=P)[:, ds(L, 1), f, :, cs]
            return v.rearrange("p a k n -> p (a k) n")

        def panel(blk, L, c, slot, ap, c0, **kw):
            v = pick(ap, L, c0, 256)
            d = raw[:, slot, :].rearrange("p (k n) -> p k n", n=256)
            load(blk, L, c, slot, [(d[:, x:x + 4], v[:, x:x + 4]) for x in (0, 4)], **kw)

        def two(blk, L, c, slot, views, **kw):
            d = raw[:, slot, :].rearrange("p (m k n) -> p m k n", m=2, n=P)
            load(blk, L, c, slot, [(d[:, m], v) for m, v in enumerate(views)], **kw)

        def down(blk, L, c0, ap, f=None):
            for n, (j, half) in enumerate(DOWN_ORDER):
                slot, k0 = (c0 + n) % RING, half * HALF_K
                v = pick(ap, L, j * P, P, f)
                d = raw[:, slot, 0:CH_DOWN].rearrange("p (k n) -> p k n", n=P)
                load(blk, L, c0 + n, slot, [(d[:, x:y], v[:, k0 + x:k0 + y]) for x, y in ((0, 6), (6, HALF_K))])

        sp.dma_start(posi[:, :], a["positions"][0:1, :].broadcast_to([P, S])).then_inc(consts_in, 16)
        sp.dma_start(const[:, :], a["const"]).then_inc(consts_in, 16)
        for h in range(2):
            sp.dma_start(xin[:, h, :], a["x"][0, h * P:(h + 1) * P, :]).then_inc(x_in, 16)
        with sp.Fori(0, DEPTH) as L:
            with sp.Fori(0, 2) as i:
                for s in range(4):
                    panel(1, L, i * 4 + s, s, a["w_in"], i * 1024 + s * 256)
            def gate(j, c):
                two(1, L, c, c % RING, [pick(a["w_in"], L, GA_COL + b * D + j * P, P) for b in range(2)])
            gate(*EARLY[0][:2])
            for n in range(2):
                c = C1["cmp"] + n
                v = a["cmp_w1"].rearrange("l t (k p) n -> p l t k n", p=P)[:, ds(L, 1), n].rearrange("p a k n -> p (a k) n")
                d = raw[:, c % RING, :].rearrange("p (k n) -> p k n", n=P)
                load(1, L, c, c % RING, [(d[:, x:x + 8], v[:, x:x + 8]) for x in (0, 8)])
            for j, c, _ in EARLY[1:]:
                gate(j, c)
            for kind, x, c, _ in BRANCH:
                if kind == "gate":
                    gate(x, c)
                else:
                    d = raw[:, c % RING, :].rearrange("p (b k n) -> p b k n", b=2, n=256)
                    load(1, L, c, c % RING, [(d[:, b], pick(a[nm], L, x * 256, 256))
                                             for b, nm in enumerate(("w_branch_a", "w_branch_b"))])
            for n in range(4):
                c = C1["out"] + n
                panel(1, L, c, c % RING, a["w_out"], n * 256)

            def up(c, slot, j):
                two(1, L, c, slot, [pick(a["ffn_w_up"], L, j + b * FF, P) for b in range(2)])
            c = C1["up"]
            with sp.Fori(0, 5) as i:
                for s in range(4):
                    up(i * 4 + (c + s), (c + s) % RING, i * 512 + s * P)
            for s in range(20, 22):
                up(c + s, (c + s) % RING, s * P)
            down(1, L, C1["down"], a["ffn_w_down"])

        with sp.Fori(0, DEPTH) as L:
            def ffn(f):
                c = C2[f"up{f}"]

                def pair(c, slot, j, lag=RING):
                    two(2, L, c, slot, [pick(a[nm], L, j, P, f) for nm in ("ffn_w_gate_2", "ffn_w_up_2")], lag=lag)
                for s in range(2):
                    pair(c + s, (c + s) % RING, s * P, lag=RING if f else 2)
                with sp.Fori(0, 5) as i:
                    for s in range(2, 6):
                        pair(i * 4 + (c + s), (c + s) % RING, i * 512 + s * P)
                down(2, L, C2[f"down{f}"], a["ffn_w_down_2"], f)

            ffn(0)
            c = C2["in"]
            with sp.Fori(0, 2) as i:
                for s in range(4):
                    panel(2, L, i * 4 + (c + s), (c + s) % RING, a["w_in_2"], i * 1024 + s * 256)
            for s in range(8, 10):
                panel(2, L, c + s, (c + s) % RING, a["w_in_2"], s * 256)
            for s in range(4):
                c = C2["out"] + s
                panel(2, L, c, c % RING, a["w_out_2"], s * 256)
            ffn(1)
        sp.wait_ge(o_rows, 4)
        sp.dma_start(out.rearrange("a (h p) n -> p (a h) n", p=P), XO[:, :, :]).then_inc(out_done, 16)
        sp.wait_ge(out_done, 16)

    @block.scalar
    def _(act):
        seq = Seq(act, act_seq)

        def f(out_, in_, func, **kw):
            if func == ACT.Copy:
                return nc.scalar.activation(out_, in_, func, **kw)
            kw.setdefault("bias", 0.0)
            kw.setdefault("scale", 1.0)
            return nc.scalar.activation(out_, in_, func, **kw)

        def split(blk, L, c_div, slot, size, part):
            if part == 0:
                act.wait_ge(landed[slot], landings(blk, L, c_div, slot))
            x, y = CUT[size][part]
            f(whi[slot][:, x:y], raw[:, slot, x:y], ACT.Copy).then_inc(whi_ready, 1)

        def split_at(blk, L, c):
            if c < len(SIZES[blk]):
                for part in range(2):
                    split(blk, L, c // RING, c % RING, SIZES[blk][c], part)

        def low_copy(t, b, n=S, scale=1.0):
            act.wait_ge(sum_ready, t + 1)
            f(low[:, b, 0:n], bank[b][:, n:2 * n], ACT.Copy, scale=scale).then_inc(low_ready, 1)

        def norm_stats(k):
            act.wait_ge(sq_used, 8 * k)
            seq.link(f(rstd[:, :], bank[4][:, 0:S], ACT.Ln, bias=col[:, 0:1]))
            f(rstd[:, :], rstd[:, :], ACT.Exp, scale=-0.5).then_inc(rstd_ready, 1)

        def square(q, src):
            if q >= 2:
                act.wait_ge(sq_used, q - 1)
            f(sq[:, q % 2, :], src, ACT.Square).then_inc(sq_ready, 1)

        def square_x(q, j):
            if j >= 4:
                act.wait_ge(sq_used, q - 3)
            f(low[:, j % 4, :], xT[:, j, :], ACT.Square).then_inc(sq_ready, 1)

        def norm_in(k, p):
            if k:
                norm_stats(k)
            for x, y in IN_GROUPS:
                act.wait_ge(h_ready, 8 * p + y)
                f(hsA[:, x:y, 0:S], Y[:, x:y, :], ACT.Copy).then_inc(hi_ready, y - x)

        def norm_out(k, p):
            norm_stats(k)
            for x, y in OUT_GROUPS:
                act.wait_ge(x_ready, 8 * p + y)
                for j in range(x, y):
                    square_x(8 * k + j, j)

        def norm_next(k):
            norm_stats(k)

        def y_stage(blk, L, c0, t0, steps, set_, gain):
            def rest(j):
                act.wait_ge(tile_out, t0 + j + 5)
                square(8 * set_ + j, Y[:, j, :])
                if j:
                    product(j - 1)

            def product(j):
                act.wait_ge(sq_ready, 8 * set_ + j + 1)
                f(Y[:, j, :], Y[:, j, :], ACT.Copy, scale=gainT[:, ds(gain + j, 1)]).then_inc(yg_ready, 1)
            done = 0
            for n in range(len(steps)):
                late = steps is DOWN and n == 2
                if not late:
                    split_at(blk, L, c0 + n + 2)
                if n == 1:
                    act.preload_act_table_set("natural_log_exp_and_others")
                for _ in range(steps[n]):
                    low_copy(t0 + done, (t0 + done) % 4)
                    if late:
                        split_at(blk, L, c0 + n + 2)
                    if done:
                        rest(done - 1)
                    done += 1
            rest(KD - 1)
            product(KD - 1)

        DOWN, OUT = [half for _, half in DOWN_ORDER], [2] * 4

        def pin(dst, src):
            act.dma_start(dst, src).then_inc(rows_in, 16)
        act.wait_ge(cleared, 1)
        for n, nm in enumerate(("attn_pre_gain", "attn_post_gain", "ffn_pre_gain", "ffn_post_gain")):
            pin(rows[16 * n:16 * n + 16, 0, :], a[nm].rearrange("l (j p) -> (l j) p", p=P))
        pin(rows[B1:B1 + 4, 0, :], a["cmp_b1"].rearrange("l t p -> (l t) p"))
        pin(rows[PSC:PSC + 4, 0, :], a["pool_scale_2"].rearrange("l (j p) -> (l j) p", p=P))
        pin(rows[CV2:CV2 + 12, 0, :], a["conv_w_2"].rearrange("l k (j p) -> (l k j) p", p=P))
        pin(rows[0:96, 1, :], a["norm_g_2"].rearrange("l g (j p) -> (l g j) p", p=P))
        for l in range(DEPTH):
            pin(rows[44 * l:44 * l + 44, 2:5, :], a["ffn_conv_w"][l].rearrange("k (j p) -> j k p", p=P))
            pin(rows[44 * l:44 * l + 44, 5, :], a["ffn_conv_b"][l].rearrange("(j p) -> j p", p=P))
        for h in range(2):
            pin(rows[:, 6, HD * h:HD * h + HD], a["cmp_pos_emb"].rearrange("l t c d -> (l t c) d"))
        act.preload_act_table_set("natural_log_exp_and_others")
        for j in range(KD):
            act.wait_ge(x_out, j // 2 + 1)
            square_x(j, j)
        norm_next(1)
        act.wait_ge(angles_ready, 1)
        f(sinT[:, :], ang[:, 3, :], ACT.Sin)
        f(cosT[:, :], ang[:, 4, :], ACT.Sin).then_inc(tables_ready, 1)
        act.drain().then_inc(layer_end, 1)

        with act.Fori(0, DEPTH) as L:
            split_at(1, L, 0)
            act.wait_ge(layer_go, L + 1)
            act.sem_inc(awake, 1)
            seq.restart(0)
            norm_in(0, 0)
            split_at(1, L, 1)
            for n in range(2):
                for h in range(2):
                    ins = f(w2cur[:, n, h, :], w2all[:, ds(L, 1), n, :].rearrange("p a d -> p (a d)"), ACT.Copy)
            ins.then_inc(cur_ready, 1)
            for c in range(12):
                split_at(1, L, c + 2)
                if c in (7, 8):
                    n = c - 7
                    act.wait_ge(cmp_in, n + 1)
                    f(RH[:, n, :, 0:30], PB[:, n, 0:480].rearrange("p (k c) -> p k c", c=30), ACT.Copy).then_inc(cmp_hi, 1)
                if c < 9 or c == 11:
                    for t in (2 * c, 2 * c + 1) if c < 9 else (EARLY[1][2], EARLY[1][2] + 1):
                        low_copy(t, t % 4)
                else:
                    t = T1["cmp"] + c - C1["cmp"]
                    low_copy(t, t % 4, n=30)
                if c == 1:
                    act.wait_ge(gates_sum, 1)
                    f(gates[:, :, :], bank[4][:, 0:48].rearrange("p (b n) -> p b n", n=24), ACT.Sigmoid).then_inc(gates_ready, 1)
                for n, (t, place) in enumerate(KEYS):
                    if t // 2 + 1 == c:
                        act.wait_ge(rope_done, ROPE.index(t) + 1)
                        f(KSW[HD:P, n, :], U1[0:HD, place, :], ACT.Copy)
                        f(KSW[0:HD, n, :], U1[HD:P, place, :], ACT.Copy).then_inc(kswap_done, 1)
                for n, t in enumerate(VALS):
                    if t // 2 + 1 == c:
                        act.wait_ge(vt_ready, n + 1)
                        f(V1[:, n, :, :], bank[6][:, 0:S].rearrange("p (b k) -> p b k", k=P), ACT.Copy).then_inc(vt_out, 1)
                if c in (9, 10):
                    n = c - C1["cmp"]
                    act.wait_ge(tile_out, T1["cmp"] + n + 5)
                    f(HC[:, n, :], HC[:, n, :], ACT.Gelu_apprx_tanh,
                      bias=gainT[:, ds(L * 2 + (B1 + n), 1)]).then_inc(cmp_hid, 1)
            act.wait_ge(cmp_kv, 1)
            act.wait_ge(tile_out, EARLY[1][2] + 2 + 4)
            f(KC[:, :], bank[6][:, 0:30], ACT.Copy)
            f(VC[0:N_CMP, :, :], bank[6][0:N_CMP, P:2 * P].rearrange("p (g d) -> p g d", g=2), ACT.Copy).then_inc(cmp_kv_out, 1)
            split_at(1, L, EARLY[2][1] + 2)
            act.wait_ge(cmp_x, 1)
            f(PC[:, :, :, 0:N_CMP], PC[:, :, :, 0:N_CMP], ACT.Exp, scale=SCALE).then_inc(cmp_e, 1)
            for t in (EARLY[2][2], EARLY[2][2] + 1):
                low_copy(t, t % 4)
            for n in range(4):
                act.wait_ge(cmp_t, n + 1)
                f(PCT[0:N_CMP, n, :], bank[4 + n][0:N_CMP, :], ACT.Copy).then_inc(cmp_t_out, 1)

            for i in range(len(MAPS) + SKEW + 3):
                m = i - SKEW - 2
                if m in LAST_MAP:
                    o = LAST_MAP.index(m)
                    g, qb, hs = UNITS[o % 6]
                    act.wait_ge(pv_done, m + 1)
                    for p in range(2):
                        dst, src = o_places(o, p)
                        ins = f(dst(0), src, ACT.Copy)
                    ins.then_inc(o_hi, 1)
                m = i - SKEW
                if 0 <= m < len(MAPS):
                    act.wait_ge(pt_ready, m + 1)
                    if m >= 2:
                        act.wait_ge(pv_done, m - 1)
                    f(PT[:, m % 2, :], bank[6 + m % 2][:, :], ACT.Copy).then_inc(pt_out, 1)
                if i < len(MAPS):
                    u, br = MAPS[i]
                    nh = len(UNITS[u][2])
                    keys = 512 // nh
                    s_ = st[:, i % 4]
                    act.wait_ge(nmax_ready, i + 1)
                    if br == 0:
                        f(s_[:, 2, 0:nh], s_[:, 2, 0:nh], ACT.Exp)
                    for x in range(nh):
                        p_ = PB[:, i % 4, x * keys:(x + 1) * keys]
                        ins = f(p_, p_, ACT.Exp, bias=s_[:, 0, x:x + 1], scale=SCALE, accum_out=s_[:, 1, x:x + 1])
                    ins.then_inc(exp_ready, 1)

            def sigmoids(j):
                g_ = gate_place(j)
                for n in range(2):
                    f(g_[:, n, :], g_[:, n, :], ACT.Sigmoid).then_inc(sg_ready, 1)
            act.wait_ge(tile_out, T1["branch"] + 4)
            for j in range(len(EARLY)):
                sigmoids(j)

            def mixed_hi(x):
                for m in range(2):
                    j = 2 * x + m
                    act.wait_ge(mix_ready, j + 1)
                    f(MS[:, j, 0:S], MX[:, m, :], ACT.Copy).then_inc(mix_hi, 1)
            for n_, (kind, x, c, t) in enumerate(BRANCH):
                split_at(1, L, c + 2)
                for n in range(2 if kind == "gate" else 4):
                    low_copy(t + n, (t + n) % 4)
                if kind == "gate":
                    act.wait_ge(tile_out, t + 2 + 4)
                    sigmoids(x)
                if n_ and BRANCH[n_ - 1][0] == "mix":
                    mixed_hi(BRANCH[n_ - 1][1])
            mixed_hi(3)
            y_stage(1, L, C1["out"], T1["out"], OUT, 0, L * 8 + G1["post"])
            norm_out(1, 0)
            norm_in(2, 1)

            def up(j, s, c_div, nslot, size, before=None):
                for n in range(2):
                    low_copy(2 * j + (T1["up"] + n), (T1["up"] + 2 * s + n) % 4)
                    split(1, L, c_div, nslot, size, n)
                    if n == 0 and before is not None:
                        act.wait_ge(conv_ready, 2 * before + 2)
                        y = CB[:, (s - 1) % 2, 0, :]
                        f(y, y, ACT.Gelu_apprx_tanh).then_inc(act_ready, 1)
                for n in range(2):
                    act.wait_ge(tile_out, 2 * j + (T1["up"] + n + 5))
                    act.wait_ge(hid_ready, j + 1)
                    k = L * 44 + j + 22 * n
                    f(CB[:, s % 2, n, :], UB[:, s % 2, n, 2:S + 2], ACT.Identity,
                      scale=convT[:, 2, ds(k, 1)], bias=convT[:, 3, ds(k, 1)]).then_inc(c0_ready, 1)
            c = C1["up"]
            act.preload_act_table_set("gelu_apprx_tanh_and_others")
            up(0, 0, (c + 2) // RING, (c + 2) % RING, CH)
            with act.Fori(0, 4) as i:
                for s in range(1, 5):
                    up(i * 4 + s, s, i + (c + s + 2) // RING, (c + s + 2) % RING, CH, i * 4 + (s - 1))
            for s in range(17, 22):
                up(s, s, (c + s + 2) // RING, (c + s + 2) % RING, SIZES[1][c + s + 2], s - 1)
            act.wait_ge(conv_ready, 2 * KF)
            f(CB[:, 1, 0, :], CB[:, 1, 0, :], ACT.Gelu_apprx_tanh).then_inc(act_ready, 1)
            y_stage(1, L, C1["down"], T1["down"], DOWN, 2, L * 8 + G1["fpost"])
            norm_out(3, 1)
            norm_next(4)
            act.drain().then_inc(layer_end, 1)

        with act.Fori(0, DEPTH) as L:
            split_at(2, L, 0)
            act.wait_ge(layer_go, L + (DEPTH + 1))
            act.sem_inc(awake, 1)
            seq.restart(0)
            def gain(g):
                return L * 48 + (NG2 + 8 * g)

            def ffn(n_ffn):
                c, t0 = C2[f"up{n_ffn}"], T2[f"up{n_ffn}"]

                def pair(j, s, c_div, nslot, size):
                    for n in range(2):
                        low_copy(2 * j + (t0 + n), (t0 + 2 * s + n) % 4)
                    split(2, L, c_div, nslot, size, 0)
                    act.wait_ge(tile_out, 2 * j + (t0 + 5))
                    act.wait_ge(hid_ready, j + (22 * n_ffn + 1))
                    f(CB[:, s % 2, 0, :], UB[:, s % 2, 0, 2:S + 2], ACT.Silu).then_inc(act_ready, 1)
                    split(2, L, c_div, nslot, size, 1)
                act.preload_act_table_set("silu_and_others")
                with act.Fori(0, 5) as i:
                    for s in range(4):
                        pair(i * 4 + s, s, i + (c + s + 2) // RING, (c + s + 2) % RING, CH)
                for s in range(20, 22):
                    pair(s, s, (c + s + 2) // RING, (c + s + 2) % RING, CH_DOWN)
                y_stage(2, L, C2[f"down{n_ffn}"], T2[f"down{n_ffn}"], DOWN, 4 * n_ffn, gain(1 + 4 * n_ffn))

            norm_in(0, 0)
            split_at(2, L, 1)
            f(parcur[:, 0:6], gainT[:, ds(L * 6 + CV2, 6)], ACT.Copy)
            f(parcur[:, 6:8], gainT[:, ds(L * 2 + PSC, 2)], ACT.Copy)
            f(poolcur[:, :, :], poolw[:, ds(L, 1), :, :].rearrange("p a n d -> p (a n) d"), ACT.Copy).then_inc(cur_ready, 1)
            ffn(0)
            norm_out(1, 0)
            norm_in(2, 1)
            for n in range(10):
                split_at(2, L, C2["in"] + n + 2)
                for t in (2 * n, 2 * n + 1):
                    low_copy(T2["in"] + t, (T2["in"] + t) % 4, scale=SCALE if t < 4 else 1.0)
                for q in range(4):
                    if (8 + q) // 2 + 1 == n:
                        act.wait_ge(vt_ready, q + 1)
                        f(V2[:, :, q * P:(q + 1) * P], bank[6 + q % 2][:, 0:S].rearrange("p (b k) -> p b k", k=P), ACT.Copy)\
                            .then_inc(vt_out, 1)
            act.preload_act_table_set("natural_log_exp_and_others")
            for i in range(8 + 3):
                if i < 8:
                    act.wait_ge(z_ready, i + 1)
                    if i >= 2:
                        act.wait_ge(sp_ready, i - 1)
                    s_ = SPA[:, i % 2, :]
                    seq.link(f(s_, z_bank(i)[:, 0:384], ACT.Abs))
                    seq.link(f(s_, s_, ACT.Exp, scale=-1.0))
                    f(s_, s_, ACT.Ln, bias=col[:, 1:2]).then_inc(ln_ready, 1)
                h = i - 1
                if 0 <= h < 8:
                    act.wait_ge(cum_ready, h + 1)
                    if h >= 2:
                        act.wait_ge(pv_done, h - 1)
                    f(AB[:, h % 2, :], z_bank(h)[:, 0:384], ACT.Exp).then_inc(ab_ready, 1)
                h = i - 3
                if 0 <= h < 8:
                    act.wait_ge(pv_done, h + 1)
                    r = HD * (h % 2)
                    f(hsA[r:r + HD, h // 2, 0:S], bank[6 + h % 2][0:HD, 0:S], ACT.Copy).then_inc(o_hi, 1)
            for n in range(2):
                act.wait_ge(sc_ready, n + 1)
                f(hsA[:, 4 + n, 0:S], U2[:, 12 + n, :], ACT.Copy).then_inc(sc_hi, 1)
            for n in range(2):
                act.wait_ge(pool_sum, n + 1)
                f(hsA[:, 6 + n, 0:S], bank[n][:, 0:S], ACT.Copy, scale=parcur[:, 6 + n:7 + n]).then_inc(sc_hi, 1)
            y_stage(2, L, C2["out"], T2["out"], OUT, 2, gain(3))
            norm_out(3, 1)
            norm_in(4, 2)
            ffn(1)
            norm_out(5, 2)
            norm_next(6)
            act.drain().then_inc(layer_end, 1)

        for n in range(2):
            act.wait_ge(o_t, n + 1)
            f(XO[:, n // 2, n % 2 * 512:n % 2 * 512 + 512], bank[n][:, :], ACT.Copy).then_inc(o_rows, 1)

    @block.vector
    def _(dve):
        seq = Seq(dve, dve_seq)
        v = nc.vector

        def split(blk, L, c, slot, size, part):
            dve.wait_ge(whi_ready, 2 * (first_chunk(blk, L) + c) + (part + 1))
            x, y = CUT[size][part]
            v.tensor_tensor(wlo[slot][:, x:y], raw[:, slot, x:y], whi[slot][:, x:y].bitcast(F32), ALU.subtract)\
                .then_inc(wlo_ready, 1)

        def split_at(blk, L, c):
            if c < len(SIZES[blk]):
                for part in range(2):
                    split(blk, L, c, c % RING, SIZES[blk][c], part)

        def tile_sum(t, b, dst, n=S, scale=1.0):
            dve.wait_ge(low_ready, t + 1)
            if scale == 1.0:
                v.tensor_tensor(dst, bank[b][:, 0:n], low[:, b, 0:n], ALU.add).then_inc(tile_out, 1)
            else:
                v.scalar_tensor_tensor(dst, bank[b][:, 0:n], scale, low[:, b, 0:n], ALU.mult, ALU.add).then_inc(tile_out, 1)

        def norm_in(k, p, gain, blk=None, L=None):
            if k:
                dve.wait_ge(rstd_ready, k)

            def lo(x, y):
                dve.wait_ge(hi_ready, 8 * p + y)
                v.tensor_tensor(hsA[:, x:y, S:2 * S], Y[:, x:y, :], hsA[:, x:y, 0:S].bitcast(F32), ALU.subtract).then_inc(hs_ready, y - x)
            for n, (x, y) in enumerate(IN_GROUPS):
                for j in range(x, y):
                    v.scalar_tensor_tensor(Y[:, j, :], xT[:, j, :], gainT[:, ds(gain + j, 1)], rstd[:, :],
                                           ALU.mult, ALU.mult).then_inc(h_ready, 1)
                if blk is not None and n < 3:
                    continue
                if blk is not None and n == 3:
                    split_at(blk, L, 0)
                    lo(*IN_GROUPS[0])
                    lo(*IN_GROUPS[1])
                if n:
                    lo(*IN_GROUPS[n - 1])
            lo(*IN_GROUPS[-1])
            dve.wait_ge(hs_ready, 8 * p + 8)

        def norm_out(k, p):
            dve.wait_ge(tile_out_now[0], tile_out_now[1])
            dve.wait_ge(rstd_ready, k)

            def add(n):
                x, y = OUT_GROUPS[n]
                dve.wait_ge(dve_seq, first + n + 1)
                v.tensor_tensor(xT[:, x:y, :], xT[:, x:y, :], Y[:, x:y, :], ALU.add).then_inc(x_ready, y - x)
            first = seq.n
            for n, (x, y) in enumerate(OUT_GROUPS):
                dve.wait_ge(yg_ready, 8 * p + y)
                v.tensor_tensor(Y[:, x:y, :], Y[:, x:y, :], rstd[:, :].unsqueeze(1).broadcast_to([P, y - x, S]), ALU.mult)\
                    .then_inc(dve_seq, 1)
                seq.n += 1
                if n:
                    add(n - 1)
            add(len(OUT_GROUPS) - 1)
            dve.wait_ge(x_ready, 8 * p + 8)

        def y_stage(blk, L, c0, t0, steps):
            done = 0
            for n in range(len(steps)):
                late = steps is DOWN and n == 2
                if not late:
                    split_at(blk, L, c0 + n + 2)
                for _ in range(steps[n]):
                    tile_sum(t0 + done, (t0 + done) % 4, Y[:, done, :])
                    done += 1
                if late:
                    split_at(blk, L, c0 + n + 2)
            tile_out_now[:] = [tile_out, t0 + done + 4]

        tile_out_now = [None, 0]
        DOWN, OUT = [half for _, half in DOWN_ORDER], [2] * 4

        def end_layer(n):
            dve.wait_ge(layer_end, n * 3)
            dve.sem_inc(awake, 1)
            dve.drain()
            dve.sem_clear(range(stage_sems[0].num, stage_sems[-1].num + 1))
            dve.sem_inc(tile_out, 4)
            dve.sem_inc(hid_ready, 2)
            dve.sem_inc(layer_go, 1)
            dve.wait_ge(layer_go, n)

        dve.sem_inc(wlo_ready, 2 * RING)
        v.memset(poolw[:, :, :, :], 0.0)
        v.memset(mean_w[:, :], 1.0 / D)
        v.memset(nones[:, :], -1.0)
        v.memset(col[:, 0:1], EPS)
        v.memset(col[:, 1:2], 1.0)
        v.memset(rows[:, :, :], 0.0).then_inc(cleared, 1)
        dve.wait_ge(consts_in, 32)
        seq.link(v.tensor_copy(ang[:, 0, :], posi[:, :]))
        seq.link(v.tensor_scalar(ang[:, 0, :], ang[:, 0, :], C("freq"), None, ALU.mult))
        for n, turn in ((3, 0.0), (4, 0.25)):
            k, r = ang[:, 1, :], ang[:, n, :]
            seq.link(v.tensor_scalar(k, ang[:, 0, :], 1.0 / TWO_PI, turn, ALU.mult, ALU.add))
            seq.link(v.tensor_scalar(k, k, ROUND, None, ALU.add))
            seq.link(v.tensor_scalar(k, k, ROUND, None, ALU.subtract))
            seq.link(v.scalar_tensor_tensor(r, k, -PI_A, ang[:, 0, :], ALU.mult, ALU.add))
            seq.link(v.scalar_tensor_tensor(r, k, -PI_B, r, ALU.mult, ALU.add))
            seq.link(v.scalar_tensor_tensor(r, k, -PI_C, r, ALU.mult, ALU.add))
            seq.link(v.tensor_scalar(r, r, turn * TWO_PI, PI_MAX, ALU.add, ALU.min))
            seq.link(v.tensor_scalar(r, r, -PI_MAX, None, ALU.max))
        dve.sem_inc(angles_ready, 1)
        for n in range(4):
            dve.wait_ge(x_t, n + 1)
            v.tensor_copy(xT[:, 2 * n:2 * n + 2, :], bank[4 + n][:, :].rearrange("p (j t) -> p j t", j=2)).then_inc(x_out, 1)
        dve.wait_ge(rows_t, 1)
        v.tensor_copy(gainT[:, 0:NG2], bank[0][:, 0:NG2])
        v.tensor_copy(gainT[:, NG2:NG2 + 96], bank[0][:, P:P + 96])
        for k in range(2):
            v.tensor_copy(convT[:, k, :], bank[0][:, (2 + k) * P:(2 + k) * P + 88])
            v.tensor_copy(convT[:, 2 + k, :], bank[1][:, k * P:k * P + 88])
        seq.link(v.tensor_copy(posT[:, :], bank[1][:, 2 * P:3 * P]))
        for l in range(DEPTH):
            for g in (1, 5):
                at = NG2 + l * 48 + g * 8
                seq.link(v.tensor_scalar(gainT[:, at:at + 8], gainT[:, at:at + 8], 0.5, None, ALU.mult))
        dve.wait_ge(tables_ready, 1)
        seq.link(v.tensor_scalar(sinT[:, :], sinT[:, :], C("sign"), None, ALU.mult))
        dve.wait_ge(params_in, 16 * N_PARAMS)
        seq.link(v.tensor_scalar(nsink[:, :, :], sink[:, :, :], -1.0, None, ALU.mult))
        end_layer(1)

        with dve.Fori(0, DEPTH) as L:
            seq.restart(0)
            norm_in(0, 0, L * 8 + G1["pre"], 1, L)
            split_at(1, L, 1)

            def rope(r):
                t = ROPE[r]
                dst = U1[:, PLACE[t], :] if t < 6 or t > 9 else QR[:, t - 6, :]
                dve.wait_ge(swap_ready, r + 1)
                v.tensor_tensor(tm[:, r % 2, :], bank[5 + 2 * (r % 2)][:, 0:S], sinT[:, :], ALU.mult).then_inc(swap_used, 1)
                dve.wait_ge(swap_used, r + 1)
                dve.wait_ge(cosmul_ready, r + 1)
                v.tensor_tensor(dst, sq[:, r % 2, :], tm[:, r % 2, :], ALU.add).then_inc(rope_done, 1)

            def cmp_build(n):
                dve.wait_ge(tile_out, T1["in"] + 10 + n + 5)
                dst = PB[:, n, 0:480].rearrange("p (k g c) -> p k g c", g=2, c=N_CMP)
                pos = posT[:, ds(L * 64 + n * 32, 32)].rearrange("p (k e) -> p k e", e=2)
                for g in range(2):
                    src = U1[HD * g:HD * g + HD, KCB + n, :].rearrange("p (c l) -> p l c", l=16)
                    for par in range(2):
                        for h in range(2):
                            ins = v.tensor_tensor(
                                dst[HD * par:HD * par + HD, 8 * h:8 * h + 8, g, :],
                                src[:, par:16:2, h:h + N_CMP],
                                pos[HD * g:HD * g + HD, 8 * h:8 * h + 8, par:par + 1].broadcast_to([HD, 8, N_CMP]), ALU.add)
                ins.then_inc(cmp_in, 1)

            def cmp_lo(n):
                dve.wait_ge(cmp_hi, n + 1)
                v.tensor_tensor(RH[:, n, :, 30:60], PB[:, n, 0:480].rearrange("p (k c) -> p k c", c=30),
                                RH[:, n, :, 0:30].bitcast(F32), ALU.subtract).then_inc(cmp_rhs, 1)

            for c in range(12):
                split_at(1, L, c + 2)
                if c in (7, 8):
                    cmp_lo(c - 7)
                if c < 8:
                    for t in (2 * c, 2 * c + 1):
                        tile_sum(t, t % 4, U1[:, PLACE[t], :])
                elif c in (8, 11):
                    j, _, t = EARLY[0 if c == 8 else 1]
                    for n in range(2):
                        tile_sum(t + n, (t + n) % 4, gate_place(j)[:, n, :])
                else:
                    n = c - C1["cmp"]
                    t = T1["cmp"] + n
                    tile_sum(t, t % 4, HC[:, n, :], n=30)
                for r, t in enumerate(ROPE):
                    if t // 2 + 1 == c:
                        rope(r)
                if c in (6, 7):
                    cmp_build(c - 6)
            split_at(1, L, EARLY[2][1] + 2)
            dve.wait_ge(gates_ready, 1)
            dve.wait_ge(cmp_z, 1)
            z = [bank[7 - 2 * par][:, 0:P].rearrange("p (b h c) -> p b h c", b=2, h=4) for par in range(2)]
            mask = C("mask_cmp").rearrange("p (b c) -> p b c", b=2)
            for qb in range(2):
                for par in range(2):
                    ins = v.tensor_tensor(PC[:, qb, par:8:2, 0:N_CMP], z[par][:, qb, :, 0:N_CMP],
                                          mask[:, qb:qb + 1, 0:N_CMP].broadcast_to([P, 4, N_CMP]), ALU.add)
            seq.link(ins)
            rowsP = PC[:, :, :, 0:N_CMP].rearrange("p b h c -> p (b h) c")

            def per_row(k):
                return stc[:, k, :].unsqueeze(2).broadcast_to([P, 16, N_CMP])
            seq.link(v.tensor_reduce(stc[:, 0, :], rowsP, AX_X, ALU.max))
            seq.link(v.tensor_scalar(stc[:, 0, :], stc[:, 0, :], 0.1 * NEG, None, ALU.max))
            v.tensor_tensor(rowsP, rowsP, per_row(0), ALU.subtract).then_inc(cmp_x, 1)
            dve.wait_ge(cmp_e, 1)
            seq.link(v.tensor_reduce(stc[:, 1, :], rowsP, AX_X, ALU.add))
            seq.link(v.tensor_scalar(stc[:, 1, :], stc[:, 1, :], TINY, None, ALU.max))
            seq.link(v.reciprocal(stc[:, 2, :], stc[:, 1, :]))
            gate = gates[:, :, :].rearrange("p b (h n) -> p (b h) n", n=3)
            seq.link(v.tensor_tensor(stc[:, 3, :], stc[:, 2, :], gate[:, :, 0], ALU.mult))
            v.tensor_tensor(rowsP, rowsP, per_row(3), ALU.mult).then_inc(cmp_p, 1)
            j, _, t = EARLY[2]
            for n in range(2):
                tile_sum(t + n, (t + n) % 4, gate_place(j)[:, n, :])

            for i in range(len(MAPS) + SKEW + 3):
                if i < len(MAPS):
                    u, br = MAPS[i]
                    g, qb, hs = UNITS[u]
                    nh = len(hs)
                    keys = 512 // nh
                    s_ = st[:, i % 4]
                    m_ = C("mask_c" if br else "mask_a")[:, (1 - qb) * P:2 * P]
                    dve.wait_ge(scores_ready, i + 1)
                    if i >= 4:
                        dve.wait_ge(pt_ready, i - 3)
                    for x in range(nh):
                        ins = v.tensor_tensor_reduce(PB[:, i % 4, x * keys:(x + 1) * keys], score_place(i, x, keys),
                                                     m_, 1.0, 3 * NEG, ALU.add, ALU.max, s_[:, 0, x:x + 1])
                    seq.link(ins)
                    if br:
                        v.tensor_scalar(s_[:, 0, 0:nh], s_[:, 0, 0:nh], -SCALE, None, ALU.mult).then_inc(nmax_ready, 1)
                    else:
                        hd = slice(hs[0], hs[0] + nh)
                        seq.link(v.scalar_tensor_tensor(s_[:, 0, 0:nh], s_[:, 0, 0:nh], -SCALE,
                                                        nsink[:, ds(L, 1), hd].rearrange("p a h -> p (a h)"), ALU.mult, ALU.min))
                        v.tensor_tensor(s_[:, 2, 0:nh], s_[:, 0, 0:nh], sink[:, ds(L, 1), hd].rearrange("p a h -> p (a h)"),
                                        ALU.add).then_inc(nmax_ready, 1)
                m = i - 1
                if 0 <= m < len(MAPS):
                    u, br = MAPS[m]
                    g, qb, hs = UNITS[u]
                    nh = len(hs)
                    s_ = st[:, m % 4]
                    dve.wait_ge(exp_ready, m + 1)
                    if br:
                        seq.link(v.tensor_scalar(s_[:, 1, 0:nh], s_[:, 1, 0:nh], TINY, None, ALU.max))
                        seq.link(v.reciprocal(s_[:, 2, 0:nh], s_[:, 1, 0:nh]))
                        v.tensor_tensor(s_[:, 3, 0:nh], s_[:, 2, 0:nh],
                                        gate[:, 8 * qb + hs[0]:8 * qb + hs[0] + nh, br], ALU.mult).then_inc(inv_ready, 1)
                    else:
                        seq.link(v.tensor_tensor(s_[:, 1, 0:nh], s_[:, 1, 0:nh], s_[:, 2, 0:nh], ALU.add))
                        v.reciprocal(s_[:, 3, 0:nh], s_[:, 1, 0:nh]).then_inc(inv_ready, 1)
                m = i - SKEW - 2
                if m in LAST_MAP:
                    o = LAST_MAP.index(m)
                    dve.wait_ge(o_hi, o + 1)
                    for p in range(2):
                        dst, src = o_places(o, p)
                        ins = v.tensor_tensor(dst(1), src, dst(0).bitcast(F32), ALU.subtract)
                    ins.then_inc(o_done, 1)

            def mixed_lo(x):
                for m in range(2):
                    j = 2 * x + m
                    dve.wait_ge(mix_hi, j + 1)
                    v.tensor_tensor(MS[:, j, S:2 * S], MX[:, m, :], MS[:, j, 0:S].bitcast(F32), ALU.subtract).then_inc(mix_split, 1)
            for n_, (kind, x, c, t) in enumerate(BRANCH):
                split_at(1, L, c + 2)
                if kind == "gate":
                    if x >= len(EARLY) + 2:
                        dve.wait_ge(mix_ready, x - 1)
                    for n in range(2):
                        tile_sum(t + n, (t + n) % 4, gate_place(x)[:, n, :])
                else:
                    if x:
                        dve.wait_ge(mix_ready, 2 * x)
                    for n in range(4):
                        tile_sum(t + n, (t + n) % 4, TA[:, n, :])
                if n_ and BRANCH[n_ - 1][0] == "mix":
                    mixed_lo(BRANCH[n_ - 1][1])
            mixed_lo(3)
            y_stage(1, L, C1["out"], T1["out"], OUT)
            norm_out(1, 0)
            norm_in(2, 1, L * 8 + G1["fpre"])

            seq.link(v.memset(UB[:, :, :, 0:2], 0.0))

            def conv(j, s):
                y = CB[:, s % 2]
                for k in (1, 0):
                    for n in range(2):
                        at = L * 44 + j + 22 * n
                        if k:
                            dve.wait_ge(c0_ready, 2 * j + (n + 1))
                        else:
                            dve.wait_ge(dve_seq, seq.base + (seq.n - 1 + n))
                        ins = v.scalar_tensor_tensor(y[:, n, :], UB[:, s % 2, n, k:S + k], convT[:, k, ds(at, 1)], y[:, n, :],
                                                     ALU.mult, ALU.add)
                        if k:
                            ins.then_inc(dve_seq, 1)
                            seq.n += 1
                        else:
                            ins.then_inc(conv_ready, 1)

            def up(j, s, c, nslot, size, before=None):
                if before is not None:
                    conv(before, s - 1)
                for n in range(2):
                    if before is not None:
                        dve.wait_ge(conv_ready, 2 * j)
                    tile_sum(2 * j + (T1["up"] + n), (T1["up"] + 2 * s + n) % 4, UB[:, s % 2, n, 2:S + 2])
                    split(1, L, c, nslot, size, n)
            c = C1["up"]
            before_up = seq.n
            up(0, 0, c + 2, (c + 2) % RING, CH)
            with dve.Fori(0, 4) as i:
                seq.restart(before_up + i * 8)
                for s in range(1, 5):
                    up(i * 4 + s, s, i * 4 + (c + s + 2), (c + s + 2) % RING, CH, i * 4 + (s - 1))
                assert seq.n == 8
            seq.restart(0)
            seq.n = before_up + 32
            for s in range(17, 22):
                up(s, s, c + s + 2, (c + s + 2) % RING, SIZES[1][c + s + 2], s - 1)
            conv(21, 21)
            y_stage(1, L, C1["down"], T1["down"], DOWN)
            norm_out(3, 1)
            end_layer(L + 2)

        with dve.Fori(0, DEPTH) as L:
            seq.restart(0)
            def gain(g):
                return L * 48 + (NG2 + 8 * g)

            def ffn(n_ffn):
                c, t0 = C2[f"up{n_ffn}"], T2[f"up{n_ffn}"]

                def pair(j, s, cc, nslot, size):
                    dve.wait_ge(hid_ready, j + (22 * n_ffn + 1))
                    for n in range(2):
                        tile_sum(2 * j + (t0 + n), (t0 + 2 * s + n) % 4, UB[:, s % 2, n, 2:S + 2])
                    split(2, L, cc, nslot, size, 0)
                    split(2, L, cc, nslot, size, 1)
                with dve.Fori(0, 5) as i:
                    for s in range(4):
                        pair(i * 4 + s, s, i * 4 + (c + s + 2), (c + s + 2) % RING, CH)
                for s in range(20, 22):
                    pair(s, s, c + s + 2, (c + s + 2) % RING, CH_DOWN)
                y_stage(2, L, C2[f"down{n_ffn}"], T2[f"down{n_ffn}"], DOWN)

            norm_in(0, 0, gain(0), 2, L)
            split_at(2, L, 1)
            ffn(0)
            norm_out(1, 0)
            norm_in(2, 1, gain(2))
            for n in range(10):
                split_at(2, L, C2["in"] + n + 2)
                for t in (2 * n, 2 * n + 1):
                    tile_sum(T2["in"] + t, (T2["in"] + t) % 4, U2[:, t, :], scale=SCALE if t < 4 else 1.0)
            for i in range(8 + 3):
                h = i
                if 0 <= h < 8:
                    dve.wait_ge(ln_ready, h + 1)
                    v.scalar_tensor_tensor(SPB[:, h % 2, :], z_bank(h)[:, 0:384], 0.0, SPA[:, h % 2, :],
                                           ALU.max, ALU.add).then_inc(sp_ready, 1)
                h = i - 3
                if 0 <= h < 8:
                    dve.wait_ge(o_hi, h + 1)
                    r = HD * (h % 2)
                    v.tensor_tensor(hsA[r:r + HD, h // 2, S:2 * S], bank[6 + h % 2][0:HD, 0:S],
                                    hsA[r:r + HD, h // 2, 0:S].bitcast(F32), ALU.subtract).then_inc(o_done, 1)
            for n in range(2):
                dve.wait_ge(sc_hi, n + 1)
                v.tensor_tensor(hsA[:, 4 + n, S:2 * S], U2[:, 12 + n, :], hsA[:, 4 + n, 0:S].bitcast(F32), ALU.subtract).then_inc(o_done, 1)
            for n in range(2):
                dve.wait_ge(sc_hi, n + 3)
                v.scalar_tensor_tensor(hsA[:, 6 + n, S:2 * S], bank[n][:, 0:S], parcur[:, 6 + n:7 + n],
                                       hsA[:, 6 + n, 0:S].bitcast(F32), ALU.mult, ALU.subtract).then_inc(o_done, 1)
            y_stage(2, L, C2["out"], T2["out"], OUT)
            norm_out(3, 1)
            norm_in(4, 2, gain(4))
            ffn(1)
            norm_out(5, 2)
            end_layer(L + 4)

        for n in range(2, 4):
            dve.wait_ge(o_t, n + 1)
            v.tensor_copy(XO[:, n // 2, n % 2 * 512:n % 2 * 512 + 512], bank[n][:, :]).then_inc(o_rows, 1)

    @block.gpsimd
    def _(pool):
        seq = Seq(pool, pool_seq)
        g_ = nc.gpsimd

        def squares(set_):
            if set_:
                pool.wait_ge(sq_used, 8 * set_)
            for j in range(1, KD - 1):
                q = 8 * set_ + j
                pool.wait_ge(sq_ready, q + 1)
                g_.tensor_tensor(sqsum[:, :], sq[:, 0, :] if j == 1 else sqsum[:, :], sq[:, q % 2, :], ALU.add)\
                    .then_inc(sq_used, 2 if j == 1 else 1)
                pool.wait_ge(sq_used, q + 1)

        def product(j, s, other, n0, t0=None):
            pool.wait_ge(hid_ready, j + (22 * n0 + 2))
            pool.wait_ge(act_ready, j + (22 * n0 + 1))
            if t0 is not None:
                pool.wait_ge(tile_out, 2 * j + (t0 + 1 + 5))
            x, y = CB[:, s % 2, 0, :], other
            dst = hid[:, ds(j, 1), :].rearrange("p a t -> p (a t)") if not isinstance(j, int) else hid[:, j, :]
            g_.tensor_tensor(HB[:, s % 2, :], x, y, ALU.mult)
            seq.link(g_.tensor_tensor(dst[:, 0:S], x, y, ALU.mult))
            g_.tensor_tensor(dst[:, S:2 * S], HB[:, s % 2, :], dst[:, 0:S].bitcast(F32), ALU.subtract).then_inc(hid_ready, 1)

        def pin(dst, src, s_):
            pool.dma_start(dst, src).then_inc(s_, 16)
        pool.wait_ge(cleared, 1)
        pin(w2all[:, :, :, :], a["cmp_w2"].rearrange("l t p d -> p l t d"), params_in)
        for l in range(DEPTH):
            pin(wg[:, l, :, :], a["w_in"][l, :, GATE_COL:GA_COL].rearrange("(k p) n -> p k n", p=P), params_in)
            pin(sink[:, l, :], a["attn_sinks"][l:l + 1, :].broadcast_to([P, 8]), params_in)
            for g in range(4):
                r = HD * (g % 2)
                pin(poolw[r:r + HD, l, g // 2, r:r + HD], a["pool_w_2"][l, g], params_in)
        pool.drain().then_inc(layer_end, 1)
        with pool.Fori(0, DEPTH) as L:
            pool.wait_ge(layer_go, L + 1)
            pool.sem_inc(awake, 1)
            seq.restart(0)
            for r, t in enumerate(ROPE):
                pool.wait_ge(tile_out, T1["in"] + t + 5)
                if r >= 2:
                    pool.wait_ge(rope_done, r - 1)
                g_.tensor_tensor(sq[:, r % 2, :], U1[:, PLACE[t], :], cosT[:, :], ALU.mult).then_inc(cosmul_ready, 1)
            for m, (u, br) in enumerate(MAPS):
                nh = len(UNITS[u][2])
                keys = 512 // nh
                pool.wait_ge(inv_ready, m + 1)
                for x in range(nh):
                    p_ = PB[:, m % 4, x * keys:(x + 1) * keys]
                    ins = g_.tensor_scalar(p_, p_, st[:, m % 4, 3, x:x + 1], 1.0, ALU.mult, ALU.mult)
                ins.then_inc(probs_ready, 1)
            for j in range(KD):
                q, m = j // 2, j % 2
                sg = gate_place(j)
                pool.wait_ge(sg_ready, 2 * j + 2)
                pool.wait_ge(tile_out, MIX_TILE[q] + 2 * m + 2 + 4)
                g_.tensor_tensor(TA[:, 2 * m, :], TA[:, 2 * m, :], sg[:, 0, :], ALU.mult)
                seq.link(g_.tensor_tensor(TA[:, 2 * m + 1, :], TA[:, 2 * m + 1, :], sg[:, 1, :], ALU.mult))
                if j >= 2:
                    pool.wait_ge(mix_split, j - 1)
                g_.tensor_tensor(MX[:, m, :], TA[:, 2 * m, :], TA[:, 2 * m + 1, :], ALU.add).then_inc(mix_ready, 1)
                pool.wait_ge(mix_ready, j + 1)
            squares(0)
            kept = seq.n
            with pool.Fori(0, 5) as i:
                seq.restart(kept + i * 4)
                for s in range(4):
                    product(i * 4 + s, s, CB[:, s % 2, 1, :], 0)
            seq.restart(0)
            seq.n = kept + 20
            for s in range(20, 22):
                product(s, s, CB[:, s % 2, 1, :], 0)
            pool.wait_ge(hid_ready, KF + 2)
            squares(2)
            pool.drain().then_inc(layer_end, 1)

        with pool.Fori(0, DEPTH) as L:
            pool.wait_ge(layer_go, L + (DEPTH + 1))
            pool.sem_inc(awake, 1)
            seq.restart(0)

            def ffn(n_ffn):
                kept = seq.n
                with pool.Fori(0, 5) as i:
                    seq.restart(kept + i * 4)
                    for s in range(4):
                        product(i * 4 + s, s, UB[:, s % 2, 1, 2:S + 2], n_ffn, T2[f"up{n_ffn}"])
                seq.restart(0)
                seq.n = kept + 20
                for s in range(20, 22):
                    product(s, s, UB[:, s % 2, 1, 2:S + 2], n_ffn, T2[f"up{n_ffn}"])
                pool.wait_ge(hid_ready, KF * (n_ffn + 1) + 2)
                squares(4 * n_ffn)
            ffn(0)
            pool.wait_ge(cur_ready, 1)
            pool.wait_ge(tile_out, T2["in"] + 20 + 4)
            seq.link(g_.memset(CU[:, :, 0:2], 0.0))
            seq.link(g_.memset(PS[:, :, 0:16], 0.0))
            for n in range(2):
                gb, y, t = U2[:, 12 + n, :], U2[:, 14 + n, :], U2[:, 16 + n, :]

                def tap(k):
                    return parcur[:, 2 * k + n:2 * k + n + 1]
                seq.link(g_.tensor_tensor(CU[:, n, 2:S + 2], y, t, ALU.mult))
                g_.tensor_scalar(y, CU[:, n, 0:S], tap(0), 1.0, ALU.mult, ALU.mult)
                seq.link(g_.tensor_scalar(t, CU[:, n, 1:S + 1], tap(1), 1.0, ALU.mult, ALU.mult))
                seq.link(g_.tensor_tensor(y, y, t, ALU.add))
                seq.link(g_.tensor_scalar(t, CU[:, n, 2:S + 2], tap(2), 1.0, ALU.mult, ALU.mult))
                seq.link(g_.tensor_tensor(y, y, t, ALU.add))
                g_.tensor_tensor(gb, gb, y, ALU.mult).then_inc(sc_ready, 1)
                pool.wait_ge(sc_ready, n + 1)
            for n in range(2):
                p_ = U2[:, 18 + n, :]
                src = p_
                seq.link(g_.tensor_copy(PS[:, 0, 16:], p_))
                for k in range(2 + 2 * n):
                    w_ = 1 << k
                    seq.link(g_.tensor_tensor(PS[:, k + 1, 16:], PS[:, k, 16:], PS[:, k, 16 - w_:16 + S - w_], ALU.add))
                d = PS[:, 0, 16:]
                cnt = C("count").rearrange("p (n c) -> p n c", n=2)
                for half in range(2):
                    rr = slice(HD * half, HD * half + HD)
                    sm = PS[rr, 1 + 2 * n + half, 16:]
                    seq.link(g_.tensor_scalar(d[rr, :], sm, C("width")[rr, n:n + 1], 1.0, ALU.mult, ALU.mult))
                    seq.link(g_.tensor_tensor(d[rr, 0:16], sm[:, 0:16], cnt[rr, n, :], ALU.mult))
                g_.tensor_tensor(p_, d, p_, ALU.subtract).then_inc(pool_in, 1)
                pool.wait_ge(pool_in, n + 1)
            squares(2)
            ffn(1)
            pool.drain().then_inc(layer_end, 1)

    @block.tensor
    def _(pe):
        mm = nc.tensor.matmul
        g32 = dict(skip_group_check=True)

        def chunk_here(blk, L, c):
            pe.wait_ge(wlo_ready, 2 * (first_chunk(blk, L) + c) + (2 * RING + 2))

        def tile(t, b, slot, ks, first=True, last=True, n=S):
            if first:
                pe.wait_ge(tile_out, t + 1)
            for x, (at, rhs, wait) in enumerate(ks):
                if wait:
                    pe.wait_ge(*wait)
                end = last and x == len(ks) - 1
                mm(bank[b][:, 0:2 * n], whi[slot][:, at:at + P], rhs[:, 0:2 * n], start=first and x == 0, stop=False, **g32)
                ins = mm(bank[b][:, n:2 * n], wlo[slot][:, at:at + P], rhs[:, 0:n], start=False, stop=end, **g32)
            if last:
                ins.then_inc(sum_ready, 1)

        def keep_warm(n):
            for _ in range(n):
                mm(bank[5][:, 0:S], ident, const[:, 0:S], start=True, stop=True, **g32)

        def norm_post(k):
            pe.wait_ge(sq_used, 8 * k + 7)
            mm(bank[4][:, 0:S], mean_w[:, :], sqsum[:, :], start=True, stop=False, **g32)
            pe.wait_ge(sq_ready, 8 * k + 8)
            mm(bank[4][:, 0:S], mean_w[:, :], sq[:, 1, :], start=False, stop=True, **g32).then_inc(sq_used, 1)
            keep_warm(6)

        def norm_pre(k):
            for j in range(KD):
                pe.wait_ge(sq_ready, 8 * k + j + 1)
                mm(bank[4][:, 0:S], mean_w[:, :], low[:, j % 4, :], start=j == 0, stop=j == KD - 1, **g32).then_inc(sq_used, 1)
            keep_warm(6)

        def hs_waits(p):
            return [(hs_ready, 8 * p + k + 1) for k in range(KD)]

        def panel(t, b, slot, rhs):
            for m in range(2):
                tile(t + m, (b + m) % 4, slot, [(k * 256 + m * P, rhs[:, k, :], None) for k in range(KD)])

        def pair(t, b, slot, rhs):
            for m in range(2):
                tile(t + m, (b + m) % 4, slot, [((m * KD + k) * P, rhs[:, k, :], None) for k in range(KD)])

        def both(t, slot, at, rhs, waits):
            pe.wait_ge(tile_out, t + 2)
            for k in range(KD):
                pe.wait_ge(*waits[k])
                for m in range(2):
                    b = (t + m) % 4
                    mm(bank[b][:, 0:2 * S], whi[slot][:, at(m, k):at(m, k) + P], rhs[:, k, :], start=k == 0, stop=False, **g32)
                    ins = mm(bank[b][:, S:2 * S], wlo[slot][:, at(m, k):at(m, k) + P], rhs[:, k, 0:S],
                             start=False, stop=k == KD - 1, **g32)
                    if k == KD - 1:
                        ins.then_inc(sum_ready, 1)

        def in_panel(m, k):
            return k * 256 + m * P

        def in_pair(m, k):
            return (m * KD + k) * P

        def down(blk, L, c0, t0, before):
            for n, (j, half) in enumerate(DOWN_ORDER):
                c, t = c0 + n, t0 + j
                chunk_here(blk, L, c)
                if n in (0, 2):
                    pe.wait_ge(hid_ready, before + (half + 1) * HALF_K + 2)
                tile(t, t % 4, c % RING, [(k * P, hid[:, half * HALF_K + k, :], None) for k in range(HALF_K)],
                     first=half == 0, last=half == 1)

        def up_pairs(blk, L, c, t, waits):
            chunk_here(blk, L, c)
            both(t, c % RING, in_pair, hsA, waits)
            with pe.Fori(0, 5) as i:
                for s in range(1, 5):
                    chunk_here(blk, L, i * 4 + (c + s))
                    pair(i * 8 + (t + 2 * s), (t + 2 * s) % 4, (c + s) % RING, hsA)
            chunk_here(blk, L, c + 21)
            pair(t + 42, (t + 42) % 4, (c + 21) % RING, hsA)

        pe.wait_ge(consts_in, 32)
        pe.wait_ge(x_in, 32)
        for n in range(4):
            for j in range(2):
                for h in range(2):
                    ins = nc.tensor.transpose(bank[4 + n][:, j * S + h * P:j * S + h * P + P],
                                              xin[:, h, (2 * n + j) * P:(2 * n + j + 1) * P], ident)
            ins.then_inc(x_t, 1)
        pe.wait_ge(cleared, 1)
        norm_pre(0)
        pe.wait_ge(rows_in, 16 * N_ROWS)
        for r in range(7):
            ins = nc.tensor.transpose(bank[r // 4][:, r % 4 * P:r % 4 * P + P], rows[:, r, :], ident)
        ins.then_inc(rows_t, 1)
        pe.drain().then_inc(layer_end, 1)

        with pe.Fori(0, DEPTH) as L:
            pe.wait_ge(layer_go, L + 1)
            pe.sem_inc(awake, 1)
            keep_warm(8)
            def gate_tiles(j, c, t):
                chunk_here(1, L, c)
                pair(t, t % 4, c % RING, hsA)
            for c in range(9):
                if c < 8:
                    chunk_here(1, L, c)
                if c == 0:
                    both(0, 0, in_panel, hsA, hs_waits(0))
                elif c == 8:
                    gate_tiles(*EARLY[0])
                else:
                    panel(2 * c, 2 * c, c % RING, hsA)
                if c == 0:
                    for b in range(2):
                        for k in range(KD):
                            ins = mm(bank[4][:, 24 * b:24 * b + 24], Y[:, k, b * P:(b + 1) * P],
                                     wg[:, ds(L, 1), k, :].rearrange("p a n -> p (a n)"),
                                     start=k == 0, stop=k == KD - 1, **g32)
                    ins.then_inc(gates_sum, 1)
                for cc in [c - 1]:
                    for t in (2 * cc, 2 * cc + 1):
                        if t in ROPE:
                            r = ROPE.index(t)
                            pe.wait_ge(tile_out, T1["in"] + t + 5)
                            if r >= 2:
                                pe.wait_ge(swap_used, r - 1)
                            mm(bank[5 + 2 * (r % 2)][:, 0:S], C("swap"), U1[:, PLACE[t], :], start=True, stop=True, **g32)\
                                .then_inc(swap_ready, 1)
                        if t in VALS:
                            n = VALS.index(t)
                            pe.wait_ge(tile_out, T1["in"] + t + 5)
                            if n:
                                pe.wait_ge(vt_out, n)
                            for b in range(2):
                                ins = nc.tensor.transpose(bank[6][:, b * P:b * P + P], U1[:, PLACE[t], b * P:b * P + P], ident)
                            ins.then_inc(vt_ready, 1)
            pe.wait_ge(cur_ready, 1)
            for n in range(2):
                c, t = C1["cmp"] + n, T1["cmp"] + n
                chunk_here(1, L, c)
                pe.wait_ge(cmp_rhs, n + 1)
                tile(t, t % 4, c % RING, [(k * P, RH[:, n, k, :], None) for k in range(16)], n=30)
            gate_tiles(*EARLY[1])
            pe.wait_ge(cmp_hid, 2)
            pe.wait_ge(vt_out, 3)
            mm(bank[6][:, 0:30], w2cur[:, 0, :, :].rearrange("p r d -> p (r d)"), HC[:, 0, :], start=True, stop=True, **g32)
            for g in range(2):
                ins = mm(bank[6][0:N_CMP, P + HD * g:P + HD * g + HD], HC[:, 1, N_CMP * g:N_CMP * g + N_CMP], w2cur[:, 1, 0, :],
                         start=True, stop=True, **g32)
            ins.then_inc(cmp_kv, 1)
            pe.wait_ge(cmp_kv_out, 1)
            pe.wait_ge(rope_done, len(ROPE))
            for qb in range(2):
                for h in range(8):
                    r, at = HD * (h % 2), (4 * qb + h // 2) * 16
                    ins = mm(bank[7 - 2 * (h % 2)][:, at:at + N_CMP], U1[r:r + HD, QB + h // 2, qb * P:qb * P + P],
                             KC[r:r + HD, N_CMP * (h // 4):N_CMP * (h // 4) + N_CMP], start=True, stop=True, **g32)
            ins.then_inc(cmp_z, 1)
            gate_tiles(*EARLY[2])
            pe.wait_ge(cmp_p, 1)
            for n in range(4):
                g, qb = n // 2, n % 2
                for x in range(4):
                    ins = nc.tensor.transpose(bank[4 + n][0:N_CMP, x * P:(x + 1) * P], PC[:, qb, 4 * g + x, 0:N_CMP], ident)
                ins.then_inc(cmp_t, 1)

            pe.wait_ge(kswap_done, 3)
            pe.wait_ge(cmp_t_out, 4)
            pe.wait_ge(tile_out, T1["branch"] + 4)
            for i in range(len(MAPS) + SKEW + 1):
                if i < len(MAPS):
                    u, br = MAPS[i]
                    g, qb, hs = UNITS[u]
                    keys = 512 // len(hs)
                    if i >= 2:
                        pe.wait_ge(nmax_ready, i - 1)
                    for x, h in enumerate(hs):
                        r = HD * (h % 2)
                        q_ = (QR if br else U1)[r:r + HD, h // 2, qb * P:qb * P + P]
                        k_ = (U1[r:r + HD, (KA, KS, KW)[br], 0:keys] if h % 2 == g else KSW[r:r + HD, br, 0:keys])
                        ins = mm(score_place(i, x, keys), q_, k_, start=True, stop=True, **g32)
                    ins.then_inc(scores_ready, 1)
                m = i - SKEW
                if 0 <= m < len(MAPS):
                    nh = len(UNITS[MAPS[m][0]][2])
                    nk = 4 // nh
                    pe.wait_ge(probs_ready, m + 1)
                    if m >= 2:
                        pe.wait_ge(pt_out, m - 1)
                    for kb in range(nk):
                        for x in range(nh):
                            ins = nc.tensor.transpose(bank[6 + m % 2][:, (kb * nh + x) * P:(kb * nh + x + 1) * P],
                                                      PB[:, m % 4, (x * nk + kb) * P:(x * nk + kb + 1) * P], ident)
                    ins.then_inc(pt_ready, 1)
                m = i - SKEW - 1
                if 0 <= m < len(MAPS):
                    u, br = MAPS[m]
                    g, qb, hs = UNITS[u]
                    nh = len(hs)
                    n = nh * P
                    o = m if br == 0 else 6 + u
                    O = bank[2 + o % 2][0:HD, 0:n]
                    pe.wait_ge(pt_out, m + 1)
                    if br < 2 and o >= 2:
                        pe.wait_ge(o_done, o - 1)
                    if br == 1:
                        x0 = (hs[0] - 4 * g) * P
                        mm(O, VC[0:N_CMP, g, :], PCT[0:N_CMP, 2 * g + qb, x0:x0 + n], start=True, stop=False, **g32)
                    for kb in range(qb + 1):
                        ins = mm(O, V1[:, br, kb, HD * g:HD * g + HD], PT[:, m % 2, kb * n:kb * n + n],
                                 start=br == 0 and kb == 0, stop=br != 1 and kb == qb, **g32)
                    ins.then_inc(pv_done, 1)

            pe.wait_ge(o_done, 12)
            for kind, x, c, t in BRANCH:
                if kind == "gate":
                    gate_tiles(x, c, t)
                else:
                    chunk_here(1, L, c)
                    for m in range(2):
                        for b in range(2):
                            tt = t + 2 * m + b
                            tile(tt, tt % 4, c % RING, [((4 * b + k) * 256 + m * P, hsB[:, 4 * b + k, :], None) for k in range(4)])
            for n in range(4):
                c, t = C1["out"] + n, T1["out"] + 2 * n
                chunk_here(1, L, c)
                if n == 0:
                    both(t, c % RING, in_panel, MS, [(mix_split, k + 1) for k in range(KD)])
                else:
                    panel(t, t % 4, c % RING, MS)
            norm_post(0)
            norm_pre(1)
            up_pairs(1, L, C1["up"], T1["up"], hs_waits(1))
            down(1, L, C1["down"], T1["down"], 0)
            norm_post(2)
            norm_pre(3)
            pe.drain().then_inc(layer_end, 1)

        with pe.Fori(0, DEPTH) as L:
            pe.wait_ge(layer_go, L + (DEPTH + 1))
            pe.sem_inc(awake, 1)
            keep_warm(8)

            def ffn(f, p):
                up_pairs(2, L, C2[f"up{f}"], T2[f"up{f}"], hs_waits(p))
                down(2, L, C2[f"down{f}"], T2[f"down{f}"], KF * f)
            ffn(0, 0)
            norm_post(0)
            norm_pre(1)
            for n in range(10):
                c, t = C2["in"] + n, T2["in"] + 2 * n
                chunk_here(2, L, c)
                if n == 0:
                    both(t, c % RING, in_panel, hsA, hs_waits(1))
                else:
                    panel(t, t % 4, c % RING, hsA)
                for q in range(4):
                    if (8 + q) // 2 + 1 == n:
                        pe.wait_ge(tile_out, T2["in"] + 8 + q + 5)
                        if q >= 2:
                            pe.wait_ge(vt_out, q - 1)
                        for b in range(2):
                            ins = nc.tensor.transpose(bank[6 + q % 2][:, b * P:b * P + P], U2[:, 8 + q, b * P:b * P + P], ident)
                        ins.then_inc(vt_ready, 1)
            pe.wait_ge(vt_out, 4)
            pe.wait_ge(tile_out, T2["in"] + 20 + 4)
            stick = C("stick")
            for i in range(8 + 2):
                if i < 8:
                    r = HD * (i % 2)
                    q_, k_ = U2[r:r + HD, i // 2, :], U2[r:r + HD, 4 + i // 2, :]
                    b_ = z_bank(i)
                    if i >= 4:
                        pe.wait_ge(ab_ready, i - 3)
                    mm(b_[:, 0:S], k_[:, 0:P], q_, start=True, stop=False, **g32)
                    mm(b_[:, S:S + P], k_[:, P:S], q_[:, P:S], start=False, stop=False, **g32)
                    mm(b_[:, 0:P], ident, stick, start=False, stop=False, **g32)
                    mm(b_[:, S:S + P], ident, stick, start=False, stop=False, **g32).then_inc(z_ready, 1)
                h = i - 1
                if 0 <= h < 8:
                    b_, s_ = z_bank(h), SPB[:, h % 2, :]
                    pe.wait_ge(sp_ready, h + 1)
                    mm(b_[:, 0:S], C("ntri"), s_[:, 0:S], start=False, stop=False, **g32)
                    mm(b_[:, S:S + P], C("ntri"), s_[:, S:S + P], start=False, stop=False, **g32)
                    mm(b_[:, P:S], nones[:, :], s_[:, S:S + P], start=False, stop=True, **g32).then_inc(cum_ready, 1)
                h = i - 2
                if 0 <= h < 8:
                    pe.wait_ge(ab_ready, h + 1)
                    if h >= 2:
                        pe.wait_ge(o_done, h - 1)
                    b_ = bank[6 + h % 2]
                    mm(b_[0:HD, 0:S], V2[:, 0, h * HD:h * HD + HD], AB[:, h % 2, 0:S], start=True, stop=False, **g32)
                    mm(b_[0:HD, P:S], V2[:, 1, h * HD:h * HD + HD], AB[:, h % 2, S:S + P], start=False, stop=True, **g32)\
                        .then_inc(pv_done, 1)
            for n in range(2):
                pe.wait_ge(pool_in, n + 1)
                mm(bank[n][:, 0:S], poolcur[:, n, :], U2[:, 18 + n, :], start=True, stop=True, **g32).then_inc(pool_sum, 1)
            pe.wait_ge(o_done, 12)
            for n in range(4):
                c, t = C2["out"] + n, T2["out"] + 2 * n
                chunk_here(2, L, c)
                panel(t, t % 4, c % RING, hsA)
            norm_post(2)
            norm_pre(3)
            ffn(1, 2)
            norm_post(4)
            norm_pre(5)
            pe.drain().then_inc(layer_end, 1)

        pe.wait_ge(layer_go, 2 * DEPTH + 1)
        for n in range(4):
            for j in range(4):
                k = 4 * (n % 2) + j
                ins = nc.tensor.transpose(bank[n][:, j * P:(j + 1) * P], xT[:, k, n // 2 * P:n // 2 * P + P], ident)
            ins.then_inc(o_t, 1)

    ctx.close()


N_ROWS = 4 + 4 + 4 + 2
N_PARAMS = 1 + 2 * 6
INPUTS = ["x", "positions", "attn_pre_gain", "attn_post_gain", "ffn_pre_gain", "ffn_post_gain", "w_in", "attn_sinks",
          "cmp_pos_emb", "cmp_w1", "cmp_b1", "cmp_w2", "w_branch_a", "w_branch_b", "w_out", "ffn_w_up", "ffn_conv_w",
          "ffn_conv_b", "ffn_w_down", "norm_g_2", "ffn_w_gate_2", "ffn_w_up_2", "ffn_w_down_2", "w_in_2", "conv_w_2",
          "pool_w_2", "pool_scale_2", "w_out_2"]


def kernel(**inputs):
    from concourse import bacc
    from concourse.bass_utils import run_bass_kernel_spmd

    nc = bacc.Bacc("TRN2", target_bir_lowering=False, num_devices=1)
    arrays = {n: np.ascontiguousarray(inputs[n]) for n in INPUTS}
    arrays["const"] = host_constants()
    handles = {n: nc.dram_tensor(f"in_{n}", v.shape, mybir.dt.from_np(v.dtype), kind="ExternalInput").ap()
               for n, v in arrays.items()}
    out = nc.dram_tensor("result", (1, S, D), F32, kind="ExternalOutput").ap()
    build(nc, handles, out)
    got = run_bass_kernel_spmd(nc, [{f"in_{n}": v for n, v in arrays.items()}], core_ids=[0])
    return got.results[0]["result"]
```
